# Optimizing a Trainium2 kernel written in Bass

```python
import numpy as np
import jax
import jax.numpy as jnp
from jax import lax

D_MODEL = 1024
BATCH = 1
SEQ = 1024
DEPTH = 1
DEC_BATCH = 8
DEC_SEQ = 4
PAST_LEN = 1024
PAGE_SIZE = 128

HEAD_DIM = 64
A_HEADS = 8
A_KV_HEADS = 2
A_GROUP = A_HEADS // A_KV_HEADS
IDX_HEADS = 8
IDX_DIM = 64
TOPK_MAX = 256
B_HEADS = 4
N_GROUPS = 3
DILATED_GROUPS = ((128, 1), (512, 4), (2048, 16))
MEM_TOKENS = 256
MEM_HEADS = 4
D_FF = ((8 * D_MODEL // 3 + 255) // 256) * 256
ROPE_THETA = 10000.0
RMS_EPS = 1e-6
BLOCK_Q = 128

A_Q = A_HEADS * HEAD_DIM
A_KV = A_KV_HEADS * HEAD_DIM
IDX_Q = IDX_HEADS * IDX_DIM
B_W = B_HEADS * HEAD_DIM
MEM_W = MEM_HEADS * HEAD_DIM
IN_SPLITS = (A_Q, A_KV, A_KV, IDX_Q, IDX_DIM, IDX_HEADS) + (B_W,) * (3 * N_GROUPS) + (D_MODEL, D_MODEL)
D_IN = sum(IN_SPLITS)
SPLIT_OFFSETS = tuple(int(c) for c in np.cumsum(IN_SPLITS)[:-1])
ATTN_SCALE = HEAD_DIM ** -0.5
IDX_SCALE = (IDX_HEADS * IDX_DIM) ** -0.5

kernel_name = "hybrid_dsa_dilated_gated_decoder_step"

def rms_norm(x, g):
    xf = x.astype(jnp.float32)
    y = xf * lax.rsqrt(jnp.mean(xf * xf, axis=-1, keepdims=True) + RMS_EPS)
    return (y * g.astype(jnp.float32)).astype(x.dtype)

def rotary(x, pos):
    half = x.shape[-1] // 2
    inv = ROPE_THETA ** (-jnp.arange(half, dtype=jnp.float32) / half)
    ang = pos.astype(jnp.float32)[:, None] * inv[None, :]
    cos = jnp.cos(ang)[:, None, :]
    sin = jnp.sin(ang)[:, None, :]
    x1 = x[..., :half].astype(jnp.float32)
    x2 = x[..., half:].astype(jnp.float32)
    return jnp.concatenate([x1 * cos - x2 * sin, x2 * cos + x1 * sin], axis=-1).astype(x.dtype)

def heads(a, n, d):
    return a.reshape(a.shape[0], a.shape[1], n, d)

def project(h, g, w_in_l, pos):
    z = rms_norm(h, g) @ w_in_l
    parts = jnp.split(z, SPLIT_OFFSETS, axis=-1)
    qa = rotary(heads(parts[0], A_HEADS, HEAD_DIM), pos)
    ka = rotary(heads(parts[1], A_KV_HEADS, HEAD_DIM), pos)
    va = heads(parts[2], A_KV_HEADS, HEAD_DIM)
    qi = rotary(heads(parts[3], IDX_HEADS, IDX_DIM), pos)
    ki = rotary(heads(parts[4], 1, IDX_DIM), pos)[:, :, 0]
    wi = parts[5]
    grp = []
    for gi in range(N_GROUPS):
        qb = rotary(heads(parts[6 + 3 * gi], B_HEADS, HEAD_DIM), pos)
        kb = rotary(heads(parts[7 + 3 * gi], B_HEADS, HEAD_DIM), pos)
        vb = heads(parts[8 + 3 * gi], B_HEADS, HEAD_DIM)
        grp.append((qb, kb, vb))
    gate_a = parts[6 + 3 * N_GROUPS]
    gate_b = parts[7 + 3 * N_GROUPS]
    return qa, ka, va, qi, ki, wi, grp, gate_a, gate_b

def indexer_scores(qi, wi, ki):
    dots = jnp.einsum('bqhd,bsd->bqhs', qi, ki).astype(jnp.float32)
    return jnp.einsum('bqh,bqhs->bqs', wi.astype(jnp.float32) * IDX_SCALE, jax.nn.relu(dots))

def sparse_attend(q, k_sel, v_sel, valid):
    b_, tq = q.shape[:2]
    qg = q.reshape(b_, tq, A_KV_HEADS, A_GROUP, HEAD_DIM)
    s = jnp.einsum('bqhgd,bqkhd->bqhgk', qg, k_sel).astype(jnp.float32) * ATTN_SCALE
    s = jnp.where(valid[:, :, None, None, :], s, -jnp.inf)
    p = jax.nn.softmax(s, axis=-1)
    o = jnp.einsum('bqhgk,bqkhd->bqhgd', p.astype(v_sel.dtype), v_sel)
    return o.reshape(b_, tq, A_Q)

def dsa_prompt(qa, ka, va, qi, ki, wi):
    b_, t_ = qa.shape[:2]
    topk = min(TOPK_MAX, t_ // 4)
    nb = t_ // BLOCK_Q
    kv = jnp.stack([ka, va], axis=2)
    key_pos = jnp.arange(t_)

    def to_blocks(a):
        return jnp.moveaxis(a.reshape((b_, nb, BLOCK_Q) + a.shape[2:]), 1, 0)

    def block_fn(args):
        qa_b, qi_b, wi_b, start = args
        qpos = start + jnp.arange(BLOCK_Q)
        sc = indexer_scores(qi_b, wi_b, ki)
        sc = jnp.where((key_pos[None, :] <= qpos[:, None])[None], sc, -jnp.inf)
        _, sel = lax.top_k(sc, topk)
        kv_sel = jax.vmap(lambda rows, ids: rows[ids])(kv, sel)
        valid = sel <= qpos[None, :, None]
        return sparse_attend(qa_b, kv_sel[:, :, :, 0], kv_sel[:, :, :, 1], valid)

    out = lax.map(block_fn, (to_blocks(qa), to_blocks(qi), to_blocks(wi), jnp.arange(nb) * BLOCK_Q))
    return jnp.moveaxis(out, 0, 1).reshape(b_, t_, A_Q)

def dsa_sample(qa, ka, va, qi, ki, wi, pool_kv, pool_idx, page_table):
    db, tn = qa.shape[:2]
    past = page_table.shape[1] * PAGE_SIZE
    n_keys = past + tn
    topk = min(TOPK_MAX, n_keys // 4)
    ki_past = pool_idx[page_table].reshape(db, past, IDX_DIM)
    ki_all = jnp.concatenate([ki_past, ki], axis=1)
    qpos = past + jnp.arange(tn)
    sc = indexer_scores(qi, wi, ki_all)
    sc = jnp.where((jnp.arange(n_keys)[None, :] <= qpos[:, None])[None], sc, -jnp.inf)
    _, sel = lax.top_k(sc, topk)
    in_past = sel < past
    sel_p = jnp.minimum(sel, past - 1)
    phys = jax.vmap(lambda pt, s: pt[s])(page_table, sel_p // PAGE_SIZE)
    kv_past = pool_kv[phys, sel_p % PAGE_SIZE]
    kv_new = jnp.stack([ka, va], axis=2)
    sel_n = jnp.clip(sel - past, 0, tn - 1)
    kv_cur = jax.vmap(lambda rows, ids: rows[ids])(kv_new, sel_n)
    kv_sel = jnp.where(in_past[..., None, None, None], kv_past, kv_cur)
    valid = sel <= qpos[None, :, None]
    return sparse_attend(qa, kv_sel[:, :, :, 0], kv_sel[:, :, :, 1], valid)

def dilated_prompt(q, k, v, window, dil):
    b_, t_, h_, d_ = q.shape
    m = window // dil
    n = t_ // dil
    nb = -(-n // m)
    n_pad = nb * m

    def sub(a):
        a = a.reshape(b_, n, dil, h_, d_).transpose(0, 2, 1, 3, 4)
        a = jnp.pad(a, ((0, 0), (0, 0), (0, n_pad - n), (0, 0), (0, 0)))
        return a.reshape(b_, dil, nb, m, h_, d_)

    def with_prev(a):
        prev = jnp.pad(a, ((0, 0), (0, 0), (1, 0), (0, 0), (0, 0), (0, 0)))[:, :, :-1]
        return jnp.concatenate([prev, a], axis=3)

    qs = sub(q)
    kb = with_prev(sub(k))
    vb = with_prev(sub(v))
    qi = jnp.arange(m)
    kj = jnp.arange(2 * m)
    offs = m + qi[:, None] - kj[None, :]
    band = (offs >= 0) & (offs <= m)
    key_ok = (jnp.arange(nb)[:, None, None] > 0) | (kj[None, None, :] >= m)
    mask = band[None] & key_ok
    s = jnp.einsum('brnqhd,brnkhd->brnhqk', qs, kb).astype(jnp.float32) * ATTN_SCALE
    s = jnp.where(mask[None, None, :, None], s, -jnp.inf)
    lse = jax.nn.logsumexp(s, axis=-1)
    p = jnp.exp(s - lse[..., None])
    o = jnp.einsum('brnhqk,brnkhd->brnqhd', p.astype(vb.dtype), vb)
    o = o.reshape(b_, dil, n_pad, h_, d_)[:, :, :n].transpose(0, 2, 1, 3, 4).reshape(b_, t_, h_, d_)
    lse = lse.transpose(0, 1, 2, 4, 3).reshape(b_, dil, n_pad, h_)[:, :, :n].transpose(0, 2, 1, 3).reshape(b_, t_, h_)
    return o, lse

def dilated_sample(q, k_new, v_new, buf_kv, window, dil):
    db, tn = q.shape[:2]
    lb = buf_kv.shape[1]
    m = window // dil
    kv_all = jnp.concatenate([buf_kv, jnp.stack([k_new, v_new], axis=2)], axis=1)
    idx = lb + jnp.arange(tn)[:, None] - dil * jnp.arange(m + 1)[None, :]
    valid = idx >= 0
    kv_sel = kv_all[:, jnp.maximum(idx, 0)]
    s = jnp.einsum('bqhd,bqkhd->bqhk', q, kv_sel[:, :, :, 0]).astype(jnp.float32) * ATTN_SCALE
    s = jnp.where(valid[None, :, None, :], s, -jnp.inf)
    lse = jax.nn.logsumexp(s, axis=-1)
    p = jnp.exp(s - lse[..., None])
    o = jnp.einsum('bqhk,bqkhd->bqhd', p.astype(kv_sel.dtype), kv_sel[:, :, :, 1])
    new_buf = kv_all[:, -min(window, lb + tn):]
    return o, lse, new_buf

def combine_dilated(outs, lses):
    wts = jax.nn.softmax(jnp.stack(lses, axis=0), axis=0)
    o = jnp.einsum('gbth,gbthd->bthd', wts, jnp.stack(outs, axis=0).astype(jnp.float32))
    return o.reshape(o.shape[0], o.shape[1], B_W).astype(outs[0].dtype)

def merge_branches(o_a, o_b, gate_a, gate_b, w_br_a_l, w_br_b_l, w_out_l):
    y = jax.nn.sigmoid(gate_a) * (o_a @ w_br_a_l) + jax.nn.sigmoid(gate_b) * (o_b @ w_br_b_l)
    return y @ w_out_l

def mem_project(mem, w_mem_kv_l):
    return (mem @ w_mem_kv_l).reshape(mem.shape[0], mem.shape[1], 2, MEM_HEADS, HEAD_DIM)

def mem_attend(h, mem_kv, w_mem_q_l, w_mem_o_l):
    q = heads(h @ w_mem_q_l, MEM_HEADS, HEAD_DIM)
    s = jnp.einsum('bqhd,bkhd->bhqk', q, mem_kv[:, :, 0]).astype(jnp.float32) * ATTN_SCALE
    p = jax.nn.softmax(s, axis=-1)
    o = jnp.einsum('bhqk,bkhd->bqhd', p.astype(mem_kv.dtype), mem_kv[:, :, 1])
    return o.reshape(h.shape[0], h.shape[1], MEM_W) @ w_mem_o_l

def swiglu(h, w_ffn_in_l, w_ffn_out_l):
    gu = h @ w_ffn_in_l
    return (jax.nn.silu(gu[..., :D_FF]) * gu[..., D_FF:]) @ w_ffn_out_l

def setup_inputs(seed: int = 0) -> dict:
    key = jax.random.key(seed)
    ks = jax.random.split(key, 24)
    n_pages = PAST_LEN // PAGE_SIZE
    n_used = DEC_BATCH * n_pages
    n_phys = n_used + max(1, n_used // 4)

    def nrm(k, shape, scale):
        return jax.random.normal(k, shape, jnp.float32) * scale

    def gain(k, shape):
        return 1.0 + 0.05 * jax.random.normal(k, shape, jnp.float32)

    perm = jax.random.permutation(ks[0], n_phys)
    page_table = perm[:n_used].reshape(DEC_BATCH, n_pages).astype(jnp.int32)
    return {
        "x_prompt": nrm(ks[1], (BATCH, SEQ, D_MODEL), 1.0),
        "x_sample": nrm(ks[2], (DEC_BATCH, DEC_SEQ, D_MODEL), 1.0),
        "mem_prompt": nrm(ks[3], (BATCH, MEM_TOKENS, D_MODEL), 1.0),
        "cache_attn_kv": nrm(ks[4], (DEPTH, n_phys, PAGE_SIZE, 2, A_KV_HEADS, HEAD_DIM), 1.0),
        "cache_idx_k": nrm(ks[5], (DEPTH, n_phys, PAGE_SIZE, IDX_DIM), 1.0),
        "cache_win1_kv": nrm(ks[6], (DEPTH, DEC_BATCH, min(DILATED_GROUPS[0][0], PAST_LEN), 2, B_HEADS, HEAD_DIM), 1.0),
        "cache_win2_kv": nrm(ks[7], (DEPTH, DEC_BATCH, min(DILATED_GROUPS[1][0], PAST_LEN), 2, B_HEADS, HEAD_DIM), 1.0),
        "cache_win3_kv": nrm(ks[8], (DEPTH, DEC_BATCH, min(DILATED_GROUPS[2][0], PAST_LEN), 2, B_HEADS, HEAD_DIM), 1.0),
        "cache_mem_kv": nrm(ks[9], (DEPTH, DEC_BATCH, MEM_TOKENS, 2, MEM_HEADS, HEAD_DIM), 1.0),
        "page_table": page_table,
        "g_mix": gain(ks[10], (DEPTH, D_MODEL)),
        "w_in": nrm(ks[11], (DEPTH, D_MODEL, D_IN), D_MODEL ** -0.5),
        "w_br_a": nrm(ks[12], (DEPTH, A_Q, D_MODEL), A_Q ** -0.5),
        "w_br_b": nrm(ks[13], (DEPTH, B_W, D_MODEL), B_W ** -0.5),
        "w_out": nrm(ks[14], (DEPTH, D_MODEL, D_MODEL), D_MODEL ** -0.5),
        "g_mem": gain(ks[15], (DEPTH, D_MODEL)),
        "w_mem_q": nrm(ks[16], (DEPTH, D_MODEL, MEM_W), D_MODEL ** -0.5),
        "w_mem_kv": nrm(ks[17], (DEPTH, D_MODEL, 2 * MEM_W), D_MODEL ** -0.5),
        "w_mem_o": nrm(ks[18], (DEPTH, MEM_W, D_MODEL), MEM_W ** -0.5),
        "g_ffn": gain(ks[19], (DEPTH, D_MODEL)),
        "w_ffn_in": nrm(ks[20], (DEPTH, D_MODEL, 2 * D_FF), D_MODEL ** -0.5),
        "w_ffn_out": nrm(ks[21], (DEPTH, D_FF, D_MODEL), D_FF ** -0.5),
        "g_final": gain(ks[22], (D_MODEL,)),
    }

def reference(x_prompt, x_sample, mem_prompt, cache_attn_kv, cache_idx_k, cache_win1_kv, cache_win2_kv,
              cache_win3_kv, cache_mem_kv, page_table, g_mix, w_in, w_br_a, w_br_b, w_out, g_mem, w_mem_q,
              w_mem_kv, w_mem_o, g_ffn, w_ffn_in, w_ffn_out, g_final):
    t_p = x_prompt.shape[1]
    t_s = x_sample.shape[1]
    past = page_table.shape[1] * PAGE_SIZE
    pos_p = jnp.arange(t_p)
    pos_s = past + jnp.arange(t_s)
    win_caches = (cache_win1_kv, cache_win2_kv, cache_win3_kv)
    hp = x_prompt
    hs = x_sample
    akv_p, ik_p, mkv_p, akv_s, ik_s = [], [], [], [], []
    win_p = [[] for _ in range(N_GROUPS)]
    win_s = [[] for _ in range(N_GROUPS)]
    for l in range(DEPTH):
        qa, ka, va, qi, ki, wi, grp, ga, gb = project(hp, g_mix[l], w_in[l], pos_p)
        o_a = dsa_prompt(qa, ka, va, qi, ki, wi)
        outs, lses = [], []
        for gi in range(N_GROUPS):
            qb, kb, vb = grp[gi]
            window, dil = DILATED_GROUPS[gi]
            o_g, lse_g = dilated_prompt(qb, kb, vb, window, dil)
            outs.append(o_g)
            lses.append(lse_g)
            win_p[gi].append(jnp.stack([kb, vb], axis=2)[:, -min(window, t_p):])
        o_b = combine_dilated(outs, lses)
        hp = hp + merge_branches(o_a, o_b, ga, gb, w_br_a[l], w_br_b[l], w_out[l])
        mkv = mem_project(mem_prompt, w_mem_kv[l])
        hp = hp + mem_attend(rms_norm(hp, g_mem[l]), mkv, w_mem_q[l], w_mem_o[l])
        hp = hp + swiglu(rms_norm(hp, g_ffn[l]), w_ffn_in[l], w_ffn_out[l])
        akv_p.append(jnp.stack([ka, va], axis=2))
        ik_p.append(ki)
        mkv_p.append(mkv)

        qa, ka, va, qi, ki, wi, grp, ga, gb = project(hs, g_mix[l], w_in[l], pos_s)
        o_a = dsa_sample(qa, ka, va, qi, ki, wi, cache_attn_kv[l], cache_idx_k[l], page_table)
        outs, lses = [], []
        for gi in range(N_GROUPS):
            qb, kb, vb = grp[gi]
            window, dil = DILATED_GROUPS[gi]
            o_g, lse_g, nbuf = dilated_sample(qb, kb, vb, win_caches[gi][l], window, dil)
            outs.append(o_g)
            lses.append(lse_g)
            win_s[gi].append(nbuf)
        o_b = combine_dilated(outs, lses)
        hs = hs + merge_branches(o_a, o_b, ga, gb, w_br_a[l], w_br_b[l], w_out[l])
        hs = hs + mem_attend(rms_norm(hs, g_mem[l]), cache_mem_kv[l], w_mem_q[l], w_mem_o[l])
        hs = hs + swiglu(rms_norm(hs, g_ffn[l]), w_ffn_in[l], w_ffn_out[l])
        akv_s.append(jnp.stack([ka, va], axis=2))
        ik_s.append(ki)
    y_prompt = rms_norm(hp, g_final)
    y_sample = rms_norm(hs, g_final)
    return (y_prompt, y_sample,
            jnp.stack(akv_p), jnp.stack(ik_p), jnp.stack(win_p[0]), jnp.stack(win_p[1]), jnp.stack(win_p[2]), jnp.stack(mkv_p),
            jnp.stack(akv_s), jnp.stack(ik_s), jnp.stack(win_s[0]), jnp.stack(win_s[1]), jnp.stack(win_s[2]))


_drawn_inputs = setup_inputs


def setup_inputs(seed=0):
    import zlib

    import numpy as np

    out = dict(_drawn_inputs(seed))
    spreads = {}
    factors = {'g_mem': 8.0}
    for name, (base, spread) in spreads.items():
        noise = np.random.default_rng([zlib.crc32(name.encode()), seed]).standard_normal(out[name].shape)
        drawn = base * np.exp(spread * noise) if base else spread * noise
        out[name] = jnp.asarray(drawn.astype(out[name].dtype))
    for name, factor in factors.items():
        out[name] = (out[name] * factor).astype(out[name].dtype)
    return out
```

```python
import numpy as np
import concourse.bass as bass
from concourse import mybir
from contextlib import ExitStack

F32 = mybir.dt.float32
F32R = mybir.dt.float32r
I32 = mybir.dt.int32
ALU = mybir.AluOpType
ACT = mybir.ActivationFunctionType
AX = mybir.AxisListType.X

P = 128
D = 1024
KC = D // P
SEQ = 1024
NT = SEQ // P
DB, DS = 8, 4
NS = DB * DS
T = SEQ + NS
TILES = NT + 1
TP = TILES * P
THIRD = T // 3
PAST, PAGE = 1024, 128
NPG = PAST // PAGE
HD = 64
AH, AKV = 8, 2
IH = 8
BH = 4
GROUPS = ((128, 1), (512, 4), (2048, 16))
MEMT = 256
DFF = 2816
FC = DFF // P
TOPK = 256
ROUNDS = TOPK // 8
EPS = 1e-6
ATT_SCALE = HD ** -0.5
IDX_SCALE = (IH * HD) ** -0.5

C_QA, C_KA, C_VA, C_QI, C_KI, C_WI = 0, 512, 640, 768, 1280, 1344
C_B = 1352
C_GATE = 3656
D_IN = 5704
ZB = 768

MASKED = -1.0e38
PICKED = -3.0e38
PICKED_BELOW = -2.0e38
NEG = -1.0e30

PROJ = [("qi", C_QI, 256, 4), ("qki", C_QI + 256, 328, 5), ("a0", 0, 384, 6), ("a1", 384, 384, 4)]
for _g in range(3):
    PROJ += [(f"b{_g}0", C_B + ZB * _g, 384, 6), (f"b{_g}1", C_B + ZB * _g + 384, 384, 2)]
GATES = [("gate", C_GATE + 384 * m, min(384, D_IN - C_GATE - 384 * m), 0) for m in range(6)]
COLS = PROJ + GATES
RAW = 2
NIDX = 2

STEPS = [(n, i, None) for n in range(len(PROJ)) for i in range(TILES)]
for _n in range(len(PROJ), len(COLS)):
    STEPS += [(_n, m, third) for m in range(COLS[_n][2] // P) for third in range(3)]
FIRST_STEP = [min(s for s, st in enumerate(STEPS) if st[0] == n) for n in range(len(COLS))] + [len(STEPS)]

SEL_TILES = list(range(TOPK // P, NT))
TURNS = [s for s in range(FIRST_STEP[NIDX]) if STEPS[s][0] or STEPS[s][1] in SEL_TILES]
SEL_OFF = {}
_o = 0
for _i in SEL_TILES:
    SEL_OFF[_i] = _o
    _o += (_i + 1) * P
SEL_OFF["s"] = _o
NKS = PAST + NS
SEL_COLS = _o + NKS


def constants():
    c = {}
    c["ident"] = np.eye(P, dtype=np.float32)
    half = HD // 2
    inv = (10000.0 ** (-np.arange(half) / half)).astype(np.float32)
    pos = np.concatenate([np.arange(SEQ), PAST + np.tile(np.arange(DS), DB)]).astype(np.float32)
    ang = (pos[:, None] * inv[None, :]).astype(np.float32)
    cos, sin = np.cos(ang).astype(np.float32), np.sin(ang).astype(np.float32)
    rope = np.zeros((TP, 2 * HD), np.float32)
    rope[:T] = np.concatenate([cos, cos, -sin, sin], axis=1)
    c["rope"] = rope
    q, k = np.arange(P)[:, None], np.arange(P)[None, :]
    c["tri_idx"] = np.where(k <= q, 0.0, MASKED).astype(np.float32)
    cur = np.where(k <= q, 0.0, NEG)
    prev = np.where(k >= q, 0.0, NEG)
    two = np.where((k <= q) & (k // HD == q // HD), 0.0, NEG)
    c["att_mask"] = np.concatenate([prev, cur, two], axis=1).astype(np.float32)
    b, t = np.arange(NS) // DS, np.arange(NS) % DS
    c["new_idx"] = np.where((b[:, None] == b[None]) & (t[None] <= t[:, None]), 0.0, MASKED).astype(np.float32)
    r = np.arange(2 * P)
    c["row_sel"] = (r[:, None] // IH == np.arange(NS)[None]).astype(np.float32).reshape(2, P, NS).transpose(1, 0, 2).reshape(P, 2 * NS).copy()
    c["row_exp"] = (np.arange(NS)[:, None] == r[None] // IH).astype(np.float32)
    row = np.arange(P)
    c["head_mask"] = np.concatenate([(row[:, None] % AH // 4 == np.arange(AKV)[None]), (row[:, None] % BH == np.arange(BH)[None])],
                                    axis=1).astype(np.float32)
    qb, qt = row // 16, row // 4 % DS
    win = np.zeros((P, 512), np.float32)
    win[:, 0:P] = np.where(np.arange(P)[None] >= qt[:, None], 0.0, NEG)
    same = qb[:, None] == b[None]
    win[:, 384:416] = np.where(same & (t[None] <= qt[:, None]), 0.0, NEG)
    win[:, 416:448] = win[:, 448:480] = np.where(same & (t[None] == qt[:, None]), 0.0, NEG)
    c["win_mask"] = win
    c["ones"] = np.ones((P, P), np.float32)
    return c


def alloc(nc, ctx):
    def sb(name, shape, dt=F32):
        return ctx.enter_context(nc.sbuf_tensor(name, shape, dt))

    def ps(name, shape, dt=F32):
        return ctx.enter_context(nc.psum_tensor(name, shape, dt))

    handles = []

    def sem(name):
        handles.append(nc.alloc_semaphore(name))
        return handles[-1]
    ctx.callback(lambda: (nc.clear_and_free_semaphores(handles), nc.all_engine_barrier()))
    return sb, ps, sem


def project_and_select(nc, d, sel):
    ctx = ExitStack()
    with ctx:
        sb, ps, sem = alloc(nc, ctx)
        n_hi = sb("n_hi", [P, KC, TP], F32R)
        n_lo = sb("n_lo", [P, KC, TP], F32R)
        w_raw = sb("w_raw", [P, RAW, 4, 384])
        w_hi = sb("w_hi", [P, 2, KC, 384], F32R)
        w_lo = sb("w_lo", [P, 2, KC, 384], F32R)
        x_in = sb("x_in", [P, 2, D])
        gain = sb("gain", [P, D])
        stat = sb("stat", [P, TILES, 3])
        ident = sb("ident1", [P, P])
        rope = sb("rope", [P, TILES, 2 * HD])
        z = sb("z", [P, 3, 384])
        rot = sb("rot", [P, 2, 384])
        tri = sb("tri", [P, P])
        qi_t = sb("qi_t", [P, 4, (NT - 2) * P])
        ki_t = sb("ki_t", [P, TP])
        wi = sb("wi", [P, TILES, IH])
        wi_s = sb("wi_s", [P, TILES, IH])
        relu = sb("relu", [P, 3, D])
        m8 = sb("m8", [P, 2, 8])
        pages = sb("pages", [1, DB * NPG], I32)
        new_idx = sb("new_idx", [NS, NS])
        row_sel = sb("row_sel", [P, 2, NS])
        w_rows = sb("w_rows", [P, 2])
        w_sel = sb("w_sel", [P, 2, NS])
        ki_page = gain[:, :].rearrange("p (u j e) -> p u j e", u=2, j=NPG)
        kis_t = x_in[0:HD, :, :]
        srelu = relu[:, :, :].rearrange("p a b -> p (a b)")[:, 0:2 * NKS].rearrange("p (u c) -> p u c", u=2)
        qis_t = z[0:HD, 0, 0:2 * P].rearrange("p (u c) -> p u c", u=2)
        qis_row = z[:, 1, 0:2 * HD].rearrange("p (u c) -> p u c", u=2)
        pz = ps("pz", [P, 2, 512])
        pt = ps("pt", [P, 2, 512])
        big = ps("big", [P, 2, 1024])

        s_const = sem("s_const")
        s_x = [sem(f"s_x{u}") for u in range(2)]
        s_raw = [sem(f"s_raw{u}") for u in range(RAW)]
        s_whi = sem("s_whi")
        s_wlo = sem("s_wlo")
        s_ssq = sem("s_ssq")
        s_mean = sem("s_mean")
        s_sqrt = sem("s_sqrt")
        s_dve = sem("s_dve")
        s_xn = sem("s_xn")
        s_xt = sem("s_xt")
        s_nhi = sem("s_nhi")
        s_nlo = sem("s_nlo")
        s_pad = sem("s_pad")
        s_z = sem("s_z")
        s_zev = sem("s_zev")
        s_pool = sem("s_pool")
        s_rot = sem("s_rot")
        s_store = [sem(f"s_store{u}") for u in range(3)]
        s_zt = sem("s_zt")
        s_ztev = sem("s_ztev")
        s_wi = sem("s_wi")
        s_wis = sem("s_wis")
        s_dot = sem("s_dot")
        s_relu = sem("s_relu")
        s_acc = sem("s_acc")
        s_pages = sem("s_pages")
        s_row = sem("s_row")
        s_kpage = [sem(f"s_kpage{u}") for u in range(2)]
        s_kpool = [sem(f"s_kpool{u}") for u in range(2)]
        s_kpt = sem("s_kpt")
        s_kptev = sem("s_kptev")
        s_sdot = sem("s_sdot")
        s_srelu = sem("s_srelu")
        s_qst = sem("s_qst")
        s_qstev = sem("s_qstev")
        s_wsel = sem("s_wsel")
        s_ssum = sem("s_ssum")
        s_scs = sem("s_scs")
        s_max = sem("s_max")
        s_rep = sem("s_rep")

        def load_pages(eng, b, pages_of, done):
            if b < 2:
                eng.wait_ge(s_xn, TILES)
            else:
                eng.wait_ge(s_kpt, b - 1)
            for j in pages_of:
                pg = eng.value_load(pages[0:1, b * NPG + j:b * NPG + j + 1], min_val=0, max_val=d["n_phys"] - 1)
                eng.dma_start(ki_page[:, b % 2, j, :], d["cache_idx_k"][bass.ds(pg, 1), :, :].rearrange("a p e -> (a p) e")).then_inc(done[b % 2], 16)

        def w_half(n, j):
            _, c0, nc_, _ = COLS[n]
            return d["w_in"][0, 4 * P * j:4 * P * (j + 1), c0:c0 + nc_].rearrange("(k p) c -> p k c", p=P)

        def rows(i):
            return (i * P, NS if i == NT else P)

        def stores(s):
            n, i, third = STEPS[s]
            kind, c0, ncol, _ = COLS[n]
            u = s % 3
            if third is not None:
                f = c0 - C_GATE + i * P
                return [(d["gates"][f:f + P, third * THIRD:(third + 1) * THIRD], z[:, u, 0:THIRD])]
            r0, r = rows(i)
            out = []
            samp = i == NT

            def add(dst, a, b):
                out.append((dst, z[0:r, u, a:b]))
            if kind == "qi" and samp:
                add(d["z_qi"][:, 0:256], 0, 256)
            if kind == "qki":
                add(d["new_idx_k_sample"] if samp else d["new_idx_k_prompt"][r0:r0 + r, :], 256, 320)
                if samp:
                    add(d["z_qi"][:, 256:512], 0, 256)
                    out.append((d["z_wi"], wi[0:NS, NT, :]))
            if kind == "a0":
                add(d["z_a"][r0:r0 + r, 0:384], 0, 384)
                if samp:
                    add(d["z_qa"][:, 0:384], 0, 384)
            if kind == "a1":
                add(d["z_a"][r0:r0 + r, 384:768], 0, 384)
                if samp:
                    add(d["z_qa"][:, 384:512], 0, 128)
                add(d["new_kv_sample"] if samp else d["new_kv_prompt"][r0:r0 + r, :], 128, 384)
            if kind[0] == "b":
                g, part = int(kind[1]), int(kind[2])
                add(d["z_b"][g][r0:r0 + r, 384 * part:384 * part + 384], 0, 384)
                if samp and part == 0:
                    add(d["z_qb"][g], 0, 256)
                keep = min(GROUPS[g][0], SEQ)
                o0 = r0 - (SEQ - keep)
                if not samp and o0 >= 0:
                    dst = d["new_win_prompt"][g]
                    if part == 0:
                        add(dst[o0:o0 + r, 0:128], 256, 384)
                    else:
                        add(dst[o0:o0 + r, 128:512], 0, 384)
            return out

        stored, count = [], [0, 0, 0]
        for s in range(len(STEPS)):
            count[s % 3] += 16 * len(stores(s))
            stored.append(count[s % 3])
        stored_all = list(count)

        dots = [(i, h) for i in SEL_TILES for h in range(IH)]

        with nc.Block() as block:
            @block.sync
            def _(sp):
                sp.dma_start(ident[:, :], d["ident"]).then_inc(s_const, 16)
                sp.dma_start(gain[:, :], d["g_mix"][0:1, :].rearrange("a c -> (a c)").partition_broadcast(P)).then_inc(s_const, 16)

                def load_x(i):
                    r0, r = rows(i)
                    if i >= 2:
                        sp.wait_ge(s_xn, i - 1)
                        sp.wait_ge(s_xt, i - 1)
                    src = d["x_sample"] if i == NT else d["x_prompt"][r0:r0 + r, :]
                    sp.dma_start(x_in[0:r, i % 2, :], src).then_inc(s_x[i % 2], 16)

                def load_half(n, j):
                    f = 2 * n + j
                    if f >= RAW:
                        sp.wait_ge(s_whi, f - RAW + 1)
                        sp.wait_ge(s_wlo, f - RAW + 1)
                    sp.dma_start(w_raw[:, f % RAW, :, 0:COLS[n][2]], w_half(n, j)).then_inc(s_raw[f % RAW], 16)

                load_x(0)
                load_half(0, 0)
                load_x(1)
                load_half(0, 1)
                sp.dma_start(rope[:, :, :], d["rope"].rearrange("(i p) c -> p i c", p=P)).then_inc(s_const, 16)
                sp.dma_start(tri[:, :], d["tri_idx"]).then_inc(s_const, 16)
                sp.dma_start(new_idx[:, :], d["new_idx"]).then_inc(s_const, 16)
                sp.dma_start(row_sel[:, :, :], d["row_sel"].rearrange("p (a c) -> p a c", a=2)).then_inc(s_const, 16)
                sp.dma_start(pages[:, :], d["page_table"].rearrange("b j -> (b j)").unsqueeze(0)).then_inc(s_pages, 16)
                for i in range(2, TILES):
                    load_x(i)
                    if i in (4, 7):
                        load_half(1, 0 if i == 4 else 1)
                load_half(2, 0)
                load_half(2, 1)
                sp.wait_ge(s_pages, 16)
                for b in range(2):
                    load_pages(sp, b, range(NPG // 2), s_kpage)
                last = FIRST_STEP[NIDX] - 1
                for s in (last - 2, last - 1, last):
                    sp.wait_ge(s_store[s % 3], stored[s])
                sp.wait_ge(s_zt, len(TURNS))
                zw = d["z_wi"].rearrange("(u b) h -> u (b h)", u=2)
                for u in range(2):
                    sp.dma_start(w_rows[:, u:u + 1], zw[u].unsqueeze(1)).then_inc(s_row, 16)
                    sp.dma_start(qis_row[:, u, :], d["z_qi"].rearrange("(u b) (h e) -> u (b h) e", u=2, e=HD)[u]).then_inc(s_row, 16)
                for b in range(2, DB):
                    load_pages(sp, b, range(NPG // 2), s_kpage)
                for n in range(2, len(COLS)):
                    for j in range(2):
                        if n > 2:
                            load_half(n, j)
                for u in range(3):
                    sp.wait_ge(s_store[u], stored_all[u])

            @block.scalar
            def _(act):
                def split_hi(n, j):
                    f = 2 * n + j
                    w = COLS[n][2]
                    act.wait_ge(s_raw[f % RAW], 16 * (f // RAW + 1))
                    if n >= 2:
                        act.wait_ge(s_z, FIRST_STEP[n - 1])
                    act.activation(w_hi[:, n % 2, 4 * j:4 * j + 4, 0:w], w_raw[:, f % RAW, :, 0:w], ACT.Copy).then_inc(s_whi, 1)

                def norm_stat(i):
                    r0, r = rows(i)
                    act.wait_ge(s_x[i % 2], 16 * (i // 2 + 1))
                    act.activation(relu[0:r, i % 2, :], x_in[0:r, i % 2, :], ACT.Square, accum_out=stat[0:r, i, 0:1]).then_inc(s_ssq, 1)

                def norm_root(i):
                    r0, r = rows(i)
                    act.wait_ge(s_mean, i + 1)
                    act.activation(stat[0:r, i, 1:2], stat[0:r, i, 2:3], ACT.Sqrt).then_inc(s_sqrt, 1)

                def hi_norm(i):
                    r0, r = rows(i)
                    act.wait_ge(s_xt, i + 1)
                    for u in range(2):
                        a = act.activation(n_hi[:, 4 * u:4 * u + 4, r0:r0 + r], big[:, i % 2, 512 * u:512 * u + 512].rearrange("p (k c) -> p k c", c=P)[:, :, 0:r], ACT.Copy)
                    a.then_inc(s_nhi, 1)

                def evac(s):
                    n, i, third = STEPS[s]
                    u = s % 3
                    act.wait_ge(s_z, s + 1)
                    if s >= 3 and stored[s - 3]:
                        act.wait_ge(s_store[u], stored[s - 3])
                    if third is not None:
                        act.activation(z[:, u, 0:THIRD], pz[:, s % 2, 0:THIRD], ACT.Sigmoid).then_inc(s_zev, 1)
                        return
                    w = COLS[n][2]
                    if COLS[n][0] == "qki":
                        act.activation(wi[:, i, :], pz[:, s % 2, 320:328], ACT.Copy).then_inc(s_wi, 1)
                        w = 320
                    act.activation(z[:, u, 0:w], pz[:, s % 2, 0:w], ACT.Copy).then_inc(s_zev, 1)

                def evac_t(s):
                    if s not in TURNS:
                        return
                    n, i, _ = STEPS[s]
                    q = TURNS.index(s)
                    act.wait_ge(s_zt, q + 1)
                    c0 = i * P
                    if n == 0:
                        q0 = c0 - 2 * P
                        act.activation(qi_t[:, 0:2, q0:q0 + P], pt[:, q % 2, 0:256].rearrange("p (a c) -> p a c", a=2), ACT.Copy).then_inc(s_ztev, 1)
                    else:
                        if i in SEL_TILES:
                            q0 = c0 - 2 * P
                            act.activation(qi_t[:, 2:4, q0:q0 + P], pt[:, q % 2, 0:256].rearrange("p (a c) -> p a c", a=2), ACT.Copy)
                        act.activation(ki_t[:, c0:c0 + P], pt[:, q % 2, 256:384], ACT.Copy).then_inc(s_ztev, 1)

                def store(s):
                    n, i, third = STEPS[s]
                    if third is None:
                        act.wait_ge(s_rot, s + 1)
                    else:
                        act.wait_ge(s_zev, s + 1)
                    if COLS[n][0] == "qki":
                        act.wait_ge(s_wi, i + 1)
                    for dst, src in stores(s):
                        act.dma_start(dst, src).then_inc(s_store[s % 3], 16)

                def step(s):
                    n, i, _ = STEPS[s]
                    k = s - FIRST_STEP[n]
                    last = FIRST_STEP[n + 1] - FIRST_STEP[n] - 1
                    evac(s)
                    if n + 1 < len(COLS) and k in (min(2, last), min(5, last)):
                        if last < 5:
                            if k == last:
                                split_hi(n + 1, 0)
                                split_hi(n + 1, 1)
                        else:
                            split_hi(n + 1, 0 if k == 2 else 1)
                    if 2 <= s < FIRST_STEP[NIDX]:
                        evac_t(s - 2)
                    if s >= 2:
                        store(s - 2)

                norm_stat(0)
                norm_root(0)
                split_hi(0, 0)
                norm_stat(1)
                norm_root(1)
                split_hi(0, 1)
                hi_norm(0)
                for i in range(TILES):
                    if i + 2 < TILES:
                        norm_stat(i + 2)
                        norm_root(i + 2)
                    if i + 1 < TILES:
                        hi_norm(i + 1)
                    step(i)
                for s in range(FIRST_STEP[1], FIRST_STEP[NIDX]):
                    step(s)
                for s in range(FIRST_STEP[NIDX] - 2, FIRST_STEP[NIDX]):
                    evac_t(s)
                    store(s)
                for j, (i, h) in enumerate(dots):
                    n = (i + 1) * P
                    act.wait_ge(s_dot, j + 1)
                    if j >= 3:
                        act.wait_ge(s_acc, j - 2)
                    act.activation(relu[:, j % 3, 0:n], big[:, j % 2, 0:n], ACT.Relu).then_inc(s_relu, 1)
                act.wait_ge(s_qst, 1)
                act.activation(qis_t[:, :, :], pt[0:HD, 0, 0:2 * P].rearrange("p (a c) -> p a c", a=2), ACT.Copy).then_inc(s_qstev, 1)
                for b in range(DB):
                    act.wait_ge(s_kpt, b + 1)
                    if b >= 2:
                        act.wait_ge(s_sdot, b - 1)
                    act.activation(kis_t[:, b % 2, :], big[0:HD, b % 2, :], ACT.Copy).then_inc(s_kptev, 1)
                    if b % 4 == 3:
                        u = b // 4
                        act.wait_ge(s_sdot, b + 1)
                        act.wait_ge(s_acc, len(dots))
                        act.activation(srelu[:, u, 0:PAST].rearrange("p (a c) -> p a c", a=2), pz[:, :, :], ACT.Relu)
                        act.activation(srelu[:, u, PAST:NKS], pt[:, 0, 0:NS], ACT.Relu).then_inc(s_srelu, 1)
                for s in range(FIRST_STEP[NIDX], len(STEPS)):
                    n, i, third = STEPS[s]
                    k = s - FIRST_STEP[n]
                    last = FIRST_STEP[n + 1] - FIRST_STEP[n] - 1
                    evac(s)
                    if n + 1 < len(COLS):
                        if last < 5:
                            if k == last:
                                split_hi(n + 1, 0)
                                split_hi(n + 1, 1)
                        elif k in (2, 5):
                            split_hi(n + 1, 0 if k == 2 else 1)
                    if s - 2 >= FIRST_STEP[NIDX]:
                        store(s - 2)
                for s in range(len(STEPS) - 2, len(STEPS)):
                    store(s)

            @block.gpsimd
            def _(pool):
                def split_lo(n, j):
                    f = 2 * n + j
                    w = COLS[n][2]
                    pool.wait_ge(s_whi, f + 1)
                    pool.tensor_tensor(w_lo[:, n % 2, 4 * j:4 * j + 4, 0:w], w_raw[:, f % RAW, :, 0:w],
                                       w_hi[:, n % 2, 4 * j:4 * j + 4, 0:w].bitcast(F32), ALU.subtract).then_inc(s_wlo, 1)

                done = [0]

                def rotate(s):
                    n, i, _ = STEPS[s]
                    nh = COLS[n][3]
                    u = s % 3
                    pool.wait_ge(s_zev, s + 1)
                    if s:
                        pool.wait_ge(s_rot, s)
                    zh = z[:, u, 0:nh * HD].rearrange("p (h a e) -> p h a e", h=nh, a=2)
                    a = rot[:, 0, 0:nh * HD].rearrange("p (h e) -> p h e", h=nh)
                    b = rot[:, 1, 0:nh * HD].rearrange("p (h a e) -> p h a e", h=nh, a=2)
                    cos = rope[:, i, 0:HD].unsqueeze(1).broadcast_to([P, nh, HD])
                    nsin = rope[:, i, HD:HD + 32].unsqueeze(1).broadcast_to([P, nh, 32])
                    psin = rope[:, i, HD + 32:2 * HD].unsqueeze(1).broadcast_to([P, nh, 32])
                    pool.tensor_tensor(a, z[:, u, 0:nh * HD].rearrange("p (h e) -> p h e", h=nh), cos, ALU.mult)
                    pool.tensor_tensor(b[:, :, 0, :], zh[:, :, 1, :], nsin, ALU.mult)
                    pool.tensor_tensor(b[:, :, 1, :], zh[:, :, 0, :], psin, ALU.mult).then_inc(s_pool, 1)
                    done[0] += 1
                    pool.wait_ge(s_pool, done[0])
                    add = pool.tensor_tensor(z[:, u, 0:nh * HD], rot[:, 0, 0:nh * HD], rot[:, 1, 0:nh * HD], ALU.add)
                    if COLS[n][0] == "qki":
                        add = pool.tensor_tensor(z[:, u, 320:384], rot[:, 0, 256:320], rot[:, 1, 256:320], ALU.add)
                    add.then_inc(s_rot, 1)

                pool.memset(n_hi[:, :, T:TP].bitcast(F32), 0.0)
                pool.memset(n_lo[:, :, T:TP].bitcast(F32), 0.0).then_inc(s_pad, 1)
                pool.wait_ge(s_const, 16 * 6)
                split_lo(0, 0)
                split_lo(0, 1)
                for s in range(FIRST_STEP[len(PROJ)]):
                    n, i, _ = STEPS[s]
                    if i == 3:
                        split_lo(n + 1, 0)
                    if i == 6:
                        split_lo(n + 1, 1)
                    rotate(s)
                    if s == FIRST_STEP[NIDX] - 1:
                        pool.wait_ge(s_pages, 16)
                        for b in range(DB):
                            load_pages(pool, b, range(NPG // 2, NPG), s_kpool)
                for n in range(len(PROJ) + 1, len(COLS)):
                    split_lo(n, 0)
                    split_lo(n, 1)

            @block.vector
            def _(dve):
                own = [0]

                def chain(ins):
                    own[0] += 1
                    ins.then_inc(s_dve, 1)
                    dve.wait_ge(s_dve, own[0])

                def mean(i):
                    r0, r = rows(i)
                    dve.wait_ge(s_ssq, i + 1)
                    dve.tensor_scalar(stat[0:r, i, 2:3], stat[0:r, i, 0:1], 1.0 / D, EPS, ALU.mult, ALU.add).then_inc(s_mean, 1)

                def normed(i):
                    r0, r = rows(i)
                    dve.wait_ge(s_sqrt, i + 1)
                    chain(dve.reciprocal(stat[0:r, i, 0:1], stat[0:r, i, 1:2]))
                    dve.scalar_tensor_tensor(out=x_in[0:r, i % 2, :], in0=x_in[0:r, i % 2, :], scalar=stat[0:r, i, 0:1],
                                             in1=gain[0:r, :], op0=ALU.mult, op1=ALU.mult).then_inc(s_xn, 1)

                def lo_norm(i):
                    r0, r = rows(i)
                    dve.wait_ge(s_nhi, i + 1)
                    for u in range(2):
                        a = dve.tensor_tensor(n_lo[:, 4 * u:4 * u + 4, r0:r0 + r],
                                              big[:, i % 2, 512 * u:512 * u + 512].rearrange("p (k c) -> p k c", c=P)[:, :, 0:r],
                                              n_hi[:, 4 * u:4 * u + 4, r0:r0 + r].bitcast(F32), ALU.subtract)
                    a.then_inc(s_nlo, 1)

                dve.wait_ge(s_const, 16 * 6)
                mean(0)
                normed(0)
                mean(1)
                normed(1)
                for i in range(TILES):
                    lo_norm(i)
                    if i + 2 < TILES:
                        mean(i + 2)
                        normed(i + 2)
                dve.wait_ge(s_wi, TILES)
                dve.tensor_scalar(wi_s[:, :, :], wi[:, :, :], IDX_SCALE, None, ALU.mult).then_inc(s_wis, 1)
                dve.wait_ge(s_wis, 1)
                for j, (i, h) in enumerate(dots):
                    n = (i + 1) * P
                    acc = sel[:, SEL_OFF[i]:SEL_OFF[i] + n]
                    dve.wait_ge(s_relu, j + 1)
                    if h == 0:
                        dve.tensor_scalar(acc, relu[:, j % 3, 0:n], wi_s[:, i, h:h + 1], None, ALU.mult).then_inc(s_acc, 1)
                    else:
                        dve.wait_ge(s_acc, j)
                        dve.scalar_tensor_tensor(out=acc, in0=relu[:, j % 3, 0:n], scalar=wi_s[:, i, h:h + 1], in1=acc,
                                                 op0=ALU.mult, op1=ALU.add).then_inc(s_acc, 1)
                for i in SEL_TILES:
                    diag = sel[:, SEL_OFF[i] + i * P:SEL_OFF[i] + (i + 1) * P]
                    dve.wait_ge(s_acc, len(dots))
                    last = dve.tensor_tensor(diag, diag, tri[:, :], ALU.add)
                chain(last)
                dve.wait_ge(s_row, 64)
                for u in range(2):
                    last = dve.tensor_scalar(w_sel[:, u, :], row_sel[:, u, :], w_rows[:, u:u + 1], IDX_SCALE, ALU.mult, ALU.mult)
                last.then_inc(s_wsel, 1)
                off = SEL_OFF["s"]
                for c in range(3):
                    dve.wait_ge(s_ssum, c + 1)
                    dve.tensor_copy(sel[0:NS, off + c * THIRD:off + (c + 1) * THIRD], pt[0:NS, 1, 0:THIRD]).then_inc(s_scs, 1)
                dve.wait_ge(s_scs, 3)
                new = sel[0:NS, off + PAST:off + NKS]
                chain(dve.tensor_tensor(new, new, new_idx[:, :], ALU.add))
                arrays = [("s", NS, NKS)] + [(i, P, (i + 1) * P) for i in reversed(SEL_TILES)]
                n_max = n_rep = 0
                for a in range(0, len(arrays), 2):
                    pair = arrays[a:a + 2]
                    for rnd in range(ROUNDS):
                        for u, (key, r, n) in enumerate(pair):
                            arr = sel[0:r, SEL_OFF[key]:SEL_OFF[key] + n]
                            if rnd:
                                dve.wait_ge(s_rep, n_rep - len(pair) + 1 + u)
                            dve.max(out=m8[0:r, u, :], in_=arr).then_inc(s_max, 1)
                        for u, (key, r, n) in enumerate(pair):
                            arr = sel[0:r, SEL_OFF[key]:SEL_OFF[key] + n]
                            dve.wait_ge(s_max, n_max + u + 1)
                            dve.match_replace(out=arr, in_to_replace=m8[0:r, u, :], in_values=arr, imm_value=PICKED).then_inc(s_rep, 1)
                        n_max += len(pair)
                        n_rep += len(pair)
                    dve.wait_ge(s_rep, n_rep)
                    for u, (key, r, n) in enumerate(pair):
                        arr = sel[0:r, SEL_OFF[key]:SEL_OFF[key] + n]
                        dve.tensor_scalar(arr, arr, PICKED_BELOW, NEG, ALU.is_gt, ALU.mult)

            @block.tensor
            def _(pe):
                def turn_x(i):
                    r0, r = rows(i)
                    pe.wait_ge(s_xn, i + 1)
                    if i >= 2:
                        pe.wait_ge(s_nhi, i - 1)
                        pe.wait_ge(s_nlo, i - 1)
                    for k in range(KC):
                        t = pe.transpose(big[:, i % 2, k * P:k * P + r], x_in[0:r, i % 2, k * P:(k + 1) * P], ident[0:r, 0:r])
                    t.then_inc(s_xt, 1)

                def project(s):
                    n, i, third = STEPS[s]
                    w = COLS[n][2]
                    if s == FIRST_STEP[n]:
                        pe.wait_ge(s_whi, 2 * n + 2)
                        pe.wait_ge(s_wlo, 2 * n + 2)
                    if n == 0:
                        pe.wait_ge(s_nhi, i + 1)
                        pe.wait_ge(s_nlo, i + 1)
                    if s >= 2:
                        pe.wait_ge(s_zev, s - 1)
                    if third is None:
                        out = pz[:, s % 2, 0:w]
                        for k in range(KC):
                            for p, (a, b) in enumerate(((n_hi, w_hi), (n_lo, w_hi), (n_hi, w_lo))):
                                m = pe.matmul(out, a[:, k, i * P:(i + 1) * P], b[:, n % 2, k, 0:w],
                                              start=(k == 0 and p == 0), stop=(k == KC - 1 and p == 2))
                    else:
                        out = pz[:, s % 2, 0:THIRD]
                        for k in range(KC):
                            for p, (a, b) in enumerate(((w_hi, n_hi), (w_hi, n_lo), (w_lo, n_hi))):
                                m = pe.matmul(out, a[:, n % 2, k, i * P:(i + 1) * P], b[:, k, third * THIRD:(third + 1) * THIRD],
                                              start=(k == 0 and p == 0), stop=(k == KC - 1 and p == 2))
                    m.then_inc(s_z, 1)

                def turn_z(s):
                    if s not in TURNS:
                        return
                    n, i, _ = STEPS[s]
                    q = TURNS.index(s)
                    pe.wait_ge(s_rot, s + 1)
                    if q >= 2:
                        pe.wait_ge(s_ztev, q - 1)
                    for c in range(2 + n):
                        t = pe.transpose(pt[:, q % 2, c * P:(c + 1) * P], z[:, s % 3, c * P:(c + 1) * P], ident[:, :])
                    t.then_inc(s_zt, 1)

                pe.wait_ge(s_const, 16 * 6)
                pe.wait_ge(s_pad, 1)
                turn_x(0)
                turn_x(1)
                for i in range(TILES):
                    project(i)
                    if i + 2 < TILES:
                        turn_x(i + 2)
                    if i >= 1:
                        turn_z(i - 1)
                for s in range(FIRST_STEP[1], FIRST_STEP[NIDX]):
                    project(s)
                    turn_z(s - 1)
                turn_z(FIRST_STEP[NIDX] - 1)
                pe.wait_ge(s_ztev, len(TURNS))
                for j, (i, h) in enumerate(dots):
                    n = (i + 1) * P
                    lo = (h % 2) * HD
                    if j >= 2:
                        pe.wait_ge(s_relu, j - 1)
                    for c in range(0, n, 512):
                        w = min(512, n - c)
                        m = pe.matmul(big[:, j % 2, c:c + w], qi_t[lo:lo + HD, h // 2, (i - 2) * P:(i - 1) * P],
                                      ki_t[lo:lo + HD, c:c + w], start=True, stop=True)
                    m.then_inc(s_dot, 1)
                pe.wait_ge(s_row, 64)
                for u in range(2):
                    t = pe.transpose(pt[0:HD, 0, u * P:(u + 1) * P], qis_row[:, u, :], ident[:, :])
                t.then_inc(s_qst, 1)
                pe.wait_ge(s_relu, len(dots))
                for b in range(DB + 1):
                    if b < DB:
                        pe.wait_ge(s_kpage[b % 2], 8 * NPG * (b // 2 + 1))
                        pe.wait_ge(s_kpool[b % 2], 8 * NPG * (b // 2 + 1))
                        if b >= 2:
                            pe.wait_ge(s_kptev, b - 1)
                        for j in range(NPG):
                            t = pe.transpose(big[0:HD, b % 2, j * P:(j + 1) * P], ki_page[:, b % 2, j, :], ident[:, :])
                        t.then_inc(s_kpt, 1)
                    if b >= 1:
                        c = b - 1
                        u, r = c // 4, 32 * (c % 4)
                        pe.wait_ge(s_kptev, c + 1)
                        if c == 0:
                            pe.wait_ge(s_qstev, 1)
                            pe.wait_ge(s_zev, FIRST_STEP[NIDX])
                        if c == 4:
                            pe.wait_ge(s_srelu, 1)
                        if c % 4 == 0:
                            pe.matmul(pt[:, 0, 0:NS], qis_t[:, u, :], ki_t[0:HD, SEQ:SEQ + NS], start=True, stop=True)
                        for e in range(2):
                            m = pe.matmul(pz[r:r + 32, e, :], qis_t[:, u, r:r + 32], kis_t[:, c % 2, 512 * e:512 * e + 512], start=True, stop=True)
                        m.then_inc(s_sdot, 1)
                pe.wait_ge(s_wsel, 1)
                pe.wait_ge(s_srelu, 2)
                for c in range(3):
                    if c:
                        pe.wait_ge(s_scs, c)
                    for u in range(2):
                        m = pe.matmul(pt[0:NS, 1, 0:THIRD], w_sel[:, u, :], srelu[:, u, c * THIRD:(c + 1) * THIRD], start=(u == 0), stop=(u == 1))
                    m.then_inc(s_ssum, 1)
                for s in range(FIRST_STEP[NIDX], len(STEPS)):
                    project(s)


B_JOBS = [(g, u) for g in range(3) for u in range(NT)]
A_JOBS = [(i, h) for i in range(NT) for h in range(AH)]
NB_J, NA_J = len(B_JOBS), len(A_JOBS)
JOBS = [("b", g, u) for g, u in B_JOBS] + [("a", i, h) for i, h in A_JOBS]
BR, OR = 7, 5
PAGED = 6
OBW = 264


def has_prev(g, u):
    return (g == 0 and u > 0) or (g == 1 and u % 2 == 1)


def block_rows(ap, g, u):
    dil = GROUPS[g][1]
    v = ap[0:SEQ, :].rearrange("(j r) c -> r j c", r=dil)
    if dil == 1:
        return [(0, v[0, u * P:(u + 1) * P, :])]
    if dil == 4:
        return [(0, v[u // 2, (u % 2) * P:(u % 2 + 1) * P, :])]
    return [(0, v[2 * u, :, :]), (64, v[2 * u + 1, :, :])]


def attend_prompt(nc, d, sel, oa, kv_pages):
    ctx = ExitStack()
    with ctx:
        sb, ps, sem = alloc(nc, ctx)
        ident = sb("ident2", [P, P])
        masks = sb("masks2", [P, 3 * P])
        first = sb("first2", [P, 2 * P])
        b_row = sb("b_row", [P, BR, ZB])
        qk_t = sb("qk_t", [P, 3, 4, P])
        ob_row = sb("ob_row", [P, OR, OBW])
        a_q = sb("a_q", [P, 2, 512])
        a_k = sb("a_k", [P, 2, 2, 2, HD])
        a_v = sb("a_v", [P, NT, 2 * HD])
        qa_t = [sb(f"qa_t_{x}", [P, 2, 4, P], F32R) for x in ("hi", "lo")]
        ka_t = [sb(f"ka_t_{x}", [P, 2, SEQ], F32R) for x in ("hi", "lo")]
        probs = sb("probs", [P, 3, 1024])
        probs_t = sb("probs_t", [P, 2, 1024])
        nmax = sb("nmax", [P, 2, AH])
        den = sb("den", [P, 2, AH])
        rden = sb("rden", [P, 2, AH])
        oa_row = sb("oa_row", [P, 2, 512])
        p_s = ps("p_s", [P, 2, 1024])
        p_t = ps("p_t", [P, 2, 512])
        p_o = ps("p_o", [P, 512])
        p_x = ps("p_x", [P, 512])

        pages = sb("pages2", [1, DB * NPG], I32)
        s_const = sem("a_const")
        s_pages = sem("a_pages")
        s_kv = sem("a_kv")
        s_win = sem("a_win")
        s_brow = [sem(f"a_brow{u}") for u in range(BR)]
        s_arow = [sem(f"a_arow{u}") for u in range(2)]
        s_xt = sem("a_xt")
        s_xev = sem("a_xev")
        s_xlo = sem("a_xlo")
        s_qk = sem("a_qk")
        s_sm = sem("a_sm")
        s_exp = sem("a_exp")
        s_pt = sem("a_pt")
        s_ptA = sem("a_ptA")
        s_ptD = sem("a_ptD")
        s_pv = sem("a_pv")
        s_oevB = sem("a_oevB")
        s_oevA = sem("a_oevA")
        s_ob = [sem(f"a_ob{u}") for u in range(OR)]
        s_dv = sem("a_dv")
        s_first = sem("a_first")

        NJ = len(JOBS)
        LAST = NJ + 5
        turns = {it: [] for it in range(LAST)}
        for j in range(NB_J):
            turns[max(0, j - 1)].append(("b", j))
        for i in range(NT):
            turns[NB_J + i * AH - 3] += [("q", i), ("k", i)]
        for i in range(NT):
            turns[NB_J + (i + 1) * AH + 3].append(("o", i))
        order = [t for it in range(LAST) for t in turns[it]]
        place = {t: n for n, t in enumerate(order)}
        lows = [sum(t[0] != "b" for t in order[:n + 1]) for n in range(len(order))]

        def width(j):
            kind, a, b = JOBS[j]
            return (a + 1) * P if kind == "a" else BH * (2 * P if has_prev(a, b) else P)

        second = [sum(width(k) > 512 for k in range(j + 1)) for j in range(NJ)]
        pieces = [len(block_rows(d["z_b"][0], g, u)) for g, u in B_JOBS]
        loaded_b = [16 * sum(pieces[k] for k in range(j % BR, j + 1, BR)) for j in range(NB_J)]
        stored_b = [16 * sum(pieces[k] for k in range(j % OR, j + 1, OR)) for j in range(NB_J)]

        with nc.Block() as block:
            @block.sync
            def _(sp):
                sp.dma_start(ident[:, :], d["ident"]).then_inc(s_const, 16)
                sp.dma_start(masks[:, :], d["att_mask"]).then_inc(s_const, 16)
                sp.dma_start(pages[:, :], d["page_table"].rearrange("b j -> (b j)").unsqueeze(0)).then_inc(s_pages, 16)

                def load_block(j):
                    g, u = B_JOBS[j]
                    if j >= BR:
                        sp.wait_ge(s_pv, j - BR + 2)
                    for p0, src in block_rows(d["z_b"][g], g, u):
                        sp.dma_start(b_row[p0:p0 + src.shape[0], j % BR, :], src).then_inc(s_brow[j % BR], 16)

                def load_tile(i):
                    if i >= 2:
                        sp.wait_ge(s_xt, place[("k", i - 2)] + 1)
                    rows = d["z_a"][i * P:(i + 1) * P, :]
                    sp.dma_start(a_q[:, i % 2, :], rows[:, 0:512]).then_inc(s_arow[i % 2], 16)
                    keys = rows[:, 512:640].rearrange("p (g e) -> p g e", g=2)
                    for c in range(2):
                        sp.dma_start(a_k[:, i % 2, :, c, :], keys).then_inc(s_arow[i % 2], 16)
                    sp.dma_start(a_v[:, i, :], rows[:, 640:768]).then_inc(s_arow[i % 2], 16)

                def load_page(q):
                    pg = sp.value_load(pages[0:1, q:q + 1], min_val=0, max_val=d["n_phys"] - 1)
                    sp.dma_start(kv_pages[:, q // NPG, q % NPG, :], d["cache_attn_kv"][bass.ds(pg, 1), :, :].rearrange("a p c -> (a p) c")).then_inc(s_kv, 16)

                for j in range(NB_J):
                    load_block(j)
                    if j == BR:
                        load_tile(0)
                        load_tile(1)
                sp.wait_ge(s_pages, 16)
                for i in range(2, NT):
                    load_tile(i)
                    for q in range(PAGED * NPG * (i - 2) // (NT - 2), PAGED * NPG * (i - 1) // (NT - 2)):
                        load_page(q)
                sp.wait_ge(s_kv, 16 * PAGED * NPG)
                for j in range(NB_J - OR, NB_J):
                    sp.wait_ge(s_ob[j % OR], stored_b[j])

            @block.scalar
            def _(act):
                def take_turned(t):
                    kind, i = t
                    act.wait_ge(s_xt, place[t] + 1)
                    src = p_x[:, :].rearrange("p (a c) -> p a c", c=P)
                    if kind == "b":
                        if i >= 3:
                            act.wait_ge(s_qk, i - 1)
                        o = qk_t[:, i % 3, :, :]
                    elif kind == "q":
                        if i >= 2:
                            act.wait_ge(s_qk, NB_J + (i - 1) * AH)
                        o = qa_t[0][:, i % 2, :, :]
                    elif kind == "k":
                        o, src = ka_t[0][:, :, i * P:(i + 1) * P], src[:, 0:2, :]
                    else:
                        o = oa[0][:, :, i * P:(i + 1) * P]
                    act.activation(o, src, ACT.Copy).then_inc(s_xev, 1)

                def exp(j):
                    kind, a, b = JOBS[j]
                    act.wait_ge(s_sm, j + 1)
                    u = j % 3
                    if kind == "a":
                        n = width(j)
                        act.activation(probs[:, u, 0:n], probs[:, u, 0:n], ACT.Exp, scale=-1.0,
                                       bias=nmax[:, a % 2, b:b + 1], accum_out=den[:, a % 2, b:b + 1]).then_inc(s_exp, 1)
                        return
                    w = width(j) // BH
                    for h in range(BH):
                        e = act.activation(probs[:, u, h * w:(h + 1) * w], probs[:, u, h * w:(h + 1) * w], ACT.Exp, scale=-1.0,
                                           bias=ob_row[:, j % OR, 256 + h:257 + h], accum_out=ob_row[:, j % OR, 260 + h:261 + h])
                    e.then_inc(s_exp, 1)

                def take_probs(j):
                    act.wait_ge(s_pt, j + 1)
                    if j >= 2:
                        act.wait_ge(s_pv, j - 1)
                    w = min(512, width(j))
                    act.activation(probs_t[:, j % 2, 0:w], p_t[:, 0, 0:w], ACT.Copy).then_inc(s_ptA, 1)

                def take_block(j):
                    g, u = B_JOBS[j]
                    act.wait_ge(s_pv, j + 1)
                    act.activation(ob_row[:, j % OR, 0:256], p_o[:, 0:256], ACT.Copy).then_inc(s_oevB, 1)
                    act.wait_ge(s_oevB, j + 1)
                    act.wait_ge(s_exp, j + 1)
                    for p0, dst in block_rows(d["o_b"][g], g, u):
                        act.dma_start(dst, ob_row[p0:p0 + dst.shape[0], j % OR, :]).then_inc(s_ob[j % OR], 16)

                for it in range(LAST):
                    for t in turns[it]:
                        take_turned(t)
                    if 0 <= it - 1 < NJ:
                        exp(it - 1)
                    if 0 <= it - 2 < NJ:
                        take_probs(it - 2)
                    if 0 <= it - 3 < NB_J:
                        take_block(it - 3)

            @block.gpsimd
            def _(pool):
                for g in range(3):
                    dst = d["new_win_sample"][g]
                    keep = dst.shape[1] - DS
                    have = d["cache_win"][g].shape[1]
                    new = d["z_b"][g][SEQ:T, :].rearrange("(b t) c -> b t c", t=DS)
                    pool.dma_start(dst[:, keep:keep + DS, :], new[:, :, 256:768]).then_inc(s_win, 16)
                    for b in range(DB):
                        pool.wait_ge(s_sm, NB_J + 2 * (DB * g + b))
                        pool.dma_start(dst[b, 0:keep, :], d["cache_win"][g][b, have - keep:have, :]).then_inc(s_win, 16)
                pool.wait_ge(s_win, 16 * 3 * (DB + 1))

            @block.vector
            def _(dve):
                def soft(j):
                    kind, a, b = JOBS[j]
                    dve.wait_ge(s_qk, j + 1)
                    if j >= 3:
                        dve.wait_ge(s_pt, j - 2)
                    u = j % 3
                    if kind == "a":
                        n = width(j)
                        if b == 0 and a >= 2:
                            dve.wait_ge(s_exp, NB_J + (a - 1) * AH)
                        bias = sel[:, SEL_OFF[a]:SEL_OFF[a] + n] if a in SEL_TILES else first[:, 2 * P - n:2 * P]
                        dve.tensor_tensor_reduce(out=probs[:, u, 0:n], in0=p_s[:, j % 2, 0:n], in1=bias, scale=-ATT_SCALE,
                                                 scalar=3.0e38, op0=ALU.add, op1=ALU.min, accum_out=nmax[:, a % 2, b:b + 1]).then_inc(s_sm, 1)
                        return
                    if j >= OR:
                        dve.wait_ge(s_ob[j % OR], stored_b[j - OR])
                    w = width(j) // BH
                    m0 = 2 * P if a == 2 else (0 if has_prev(a, b) else P)
                    for h in range(BH):
                        c = h % 2 * 512 + h // 2 * w
                        t = dve.tensor_tensor_reduce(out=probs[:, u, h * w:(h + 1) * w], in0=p_s[:, j % 2, c:c + w],
                                                     in1=masks[:, m0:m0 + w], scale=-ATT_SCALE, scalar=3.0e38,
                                                     op0=ALU.add, op1=ALU.min, accum_out=ob_row[:, j % OR, 256 + h:257 + h])
                    t.then_inc(s_sm, 1)

                def take_probs(j):
                    w = width(j)
                    if w <= 512:
                        return
                    dve.wait_ge(s_pt, j + 1)
                    if j >= 2:
                        dve.wait_ge(s_pv, j - 1)
                    dve.tensor_copy(probs_t[:, j % 2, 512:w], p_t[:, 1, 0:w - 512]).then_inc(s_ptD, 1)

                def normalise(i):
                    j = NB_J + i * AH + AH - 1
                    dve.wait_ge(s_exp, j + 1)
                    dve.reciprocal(rden[:, i % 2, :], den[:, i % 2, :]).then_inc(s_dv, 1)
                    dve.wait_ge(s_dv, i + 1)
                    dve.wait_ge(s_pv, j + 1)
                    if i >= 2:
                        dve.wait_ge(s_xt, place[("o", i - 2)] + 1)
                    dve.tensor_tensor(oa_row[:, i % 2, :].rearrange("p (h e) -> p h e", h=AH), p_o[:, :].rearrange("p (h e) -> p h e", h=AH),
                                      rden[:, i % 2, :].unsqueeze(2).broadcast_to([P, AH, HD]), ALU.mult).then_inc(s_oevA, 1)

                def low(t):
                    kind, i = t
                    dve.wait_ge(s_xev, place[t] + 1)
                    if kind == "q" and i >= 2:
                        dve.wait_ge(s_qk, NB_J + (i - 1) * AH)
                    hi, lo = ([x[:, i % 2, :, :] for x in qa_t] if kind == "q" else [x[:, :, i * P:(i + 1) * P] for x in (ka_t if kind == "k" else oa)])
                    src = p_x[:, :].rearrange("p (a c) -> p a c", c=P)[:, 0:hi.shape[1], :]
                    dve.tensor_tensor(lo, src, hi.bitcast(F32), ALU.subtract).then_inc(s_xlo, 1)

                dve.wait_ge(s_const, 32)
                dve.memset(first[:, 0:P], 0.0).then_inc(s_first, 1)
                dve.tensor_copy(first[:, P:2 * P], masks[:, P:2 * P]).then_inc(s_first, 1)
                dve.wait_ge(s_first, 2)
                for it in range(LAST):
                    for t in turns[it]:
                        if t[0] != "b":
                            low(t)
                    if it < NJ:
                        soft(it)
                    if 0 <= it - 2 < NJ:
                        take_probs(it - 2)
                    j = it - 3
                    if NB_J <= j < NJ and (j - NB_J) % AH == AH - 1:
                        normalise((j - NB_J) // AH)

            @block.tensor
            def _(pe):
                def turn(t):
                    kind, i = t
                    n = place[t]
                    if n:
                        pe.wait_ge(s_xev, n)
                        if lows[n - 1]:
                            pe.wait_ge(s_xlo, lows[n - 1])
                    if kind == "b":
                        pe.wait_ge(s_brow[i % BR], loaded_b[i])
                        src = [b_row[:, i % BR, c * P:(c + 1) * P] for c in range(4)]
                    elif kind == "q":
                        pe.wait_ge(s_arow[i % 2], 64 * (i // 2 + 1))
                        src = [a_q[:, i % 2, c * P:(c + 1) * P] for c in range(4)]
                    elif kind == "k":
                        src = [a_k[:, i % 2, g, :, :].rearrange("p c e -> p (c e)") for g in range(2)]
                    else:
                        pe.wait_ge(s_oevA, i + 1)
                        src = [oa_row[:, i % 2, c * P:(c + 1) * P] for c in range(4)]
                    for c, x in enumerate(src):
                        m = pe.transpose(p_x[:, c * P:(c + 1) * P], x, ident[:, :])
                    m.then_inc(s_xt, 1)

                def logits(j):
                    kind, a, b = JOBS[j]
                    if j >= 2:
                        pe.wait_ge(s_sm, j - 1)
                    if kind == "a":
                        if b == 0:
                            pe.wait_ge(s_xlo, lows[place[("k", a)]])
                        n, lo = width(j), (b % 2) * HD
                        for c in range(0, n, 512):
                            w = min(512, n - c)
                            for part, (x, y) in enumerate(((0, 0), (1, 0), (0, 1))):
                                m = pe.matmul(p_s[:, j % 2, c:c + w], qa_t[x][lo:lo + HD, a % 2, b // 2, :], ka_t[y][lo:lo + HD, b // 4, c:c + w],
                                              start=(part == 0), stop=(part == 2))
                    else:
                        pe.wait_ge(s_xev, place[("b", j)] + 1)
                        blocks = ([(j - 1) % 3] if has_prev(a, b) else []) + [j % 3]
                        for h in range(BH):
                            lo = (h % 2) * HD
                            c = h % 2 * 512 + h // 2 * P * len(blocks)
                            for kb in blocks:
                                m = pe.matmul(p_s[:, j % 2, c:c + P], qk_t[lo:lo + HD, j % 3, h // 2, :], qk_t[lo:lo + HD, kb, 2 + h // 2, :],
                                              start=True, stop=True)
                                c += P
                    m.then_inc(s_qk, 1)

                def turn_probs(j):
                    pe.wait_ge(s_exp, j + 1)
                    if j:
                        pe.wait_ge(s_ptA, j)
                        if second[j - 1]:
                            pe.wait_ge(s_ptD, second[j - 1])
                    for c in range(width(j) // P):
                        m = pe.transpose(p_t[:, c // 4, c % 4 * P:(c % 4 + 1) * P], probs[:, j % 3, c * P:(c + 1) * P], ident[:, :])
                    m.then_inc(s_pt, 1)

                def values(j):
                    kind, a, b = JOBS[j]
                    pe.wait_ge(s_ptA, j + 1)
                    if second[j]:
                        pe.wait_ge(s_ptD, second[j])
                    if kind == "a":
                        if b == 0:
                            pe.wait_ge(s_oevB, NB_J)
                            if a:
                                pe.wait_ge(s_oevA, a)
                        for c in range(a + 1):
                            m = pe.matmul(p_o[:, b * HD:(b + 1) * HD], probs_t[:, j % 2, c * P:(c + 1) * P],
                                          a_v[:, c, (b // 4) * HD:(b // 4 + 1) * HD], start=(c == 0), stop=(c == a))
                    else:
                        if j:
                            pe.wait_ge(s_oevB, j)
                        slots = ([(j - 1) % BR] if has_prev(a, b) else []) + [j % BR]
                        c = 0
                        for h in range(BH):
                            for n, v in enumerate(slots):
                                m = pe.matmul(p_o[:, h * HD:(h + 1) * HD], probs_t[:, j % 2, c * P:(c + 1) * P],
                                              b_row[:, v, 512 + h * HD:512 + (h + 1) * HD], start=(n == 0), stop=(n == len(slots) - 1))
                                c += 1
                    m.then_inc(s_pv, 1)

                pe.wait_ge(s_const, 32)
                for it in range(LAST):
                    for t in turns[it]:
                        turn(t)
                    if it < NJ:
                        logits(it)
                    if 0 <= it - 2 < NJ:
                        turn_probs(it - 2)
                    if 0 <= it - 3 < NJ:
                        values(it - 3)


def attend_sample_a(nc, d, sel, oa, ob, kv_pages):
    ctx = ExitStack()
    with ctx:
        sb, ps, sem = alloc(nc, ctx)
        ident = sb("ident3", [P, P])
        hmask = sb("hmask3", [P, AKV + BH])
        row_exp = sb("row_exp3", [NS, 2, P])
        cb = sb("cb", [P, 3, NT, OBW])
        low = sb("low", [P, NT, 2, BH])
        ex = sb("ex", [P, 3, NT, BH])
        tot = sb("tot", [P, 3, NT, BH])
        ob_row = sb("ob_row3", [P, NT, 256])
        term = sb("term3", [P, NT, 256])
        q_row = sb("q_row", [P, 2, HD])
        q_exp = sb("q_exp", [P, 2, P])
        q_t = sb("q_t", [P, 2, P])
        k_t = sb("k_t", [P, 2, PAST])
        k_new = sb("k_new", [NS, P])
        k_newt = sb("k_newt", [P, NS])
        v_new = sb("v_new", [P, P])
        kv_late = sb("kv_late", [P, DB - PAGED, NPG, 2 * P])
        pages = sb("pages3", [1, DB * NPG], I32)
        probs = sb("probs3", [P, 9 * P])
        probs_t = sb("probs_t3", [P, 9, P])
        st = sb("st3", [P, 2, 6])
        o_half = sb("o_half", [P, 2, 2, HD])
        o_row = sb("o_row3", [NS, 512])
        p_x = ps("p_x3", [P, 2, 512])
        p_s = ps("p_s3", [P, 2, 512])
        p_n = ps("p_n3", [P, 512])
        p_o = ps("p_o3", [P, 512])
        p_t = ps("p_t3", [P, 2, 512])

        s_const = sem("b_const")
        s_cb = sem("b_cb")
        s_pages = sem("b_pages")
        s_kv = [sem(f"b_kv{b}") for b in range(DB - PAGED)]
        s_q = sem("b_q")
        s_dv = sem("b_dv")
        s_diff = sem("b_diff")
        s_ex = sem("b_ex")
        s_obrow = sem("b_obrow")
        s_ct = sem("b_ct")
        s_chi = sem("b_chi")
        s_clo = sem("b_clo")
        s_qexp = sem("b_qexp")
        s_pad = sem("b_pad")
        s_qt = sem("b_qt")
        s_qtev = sem("b_qtev")
        s_kt = sem("b_kt")
        s_ktev = sem("b_ktev")
        s_qk = sem("b_qk")
        s_sm = sem("b_sm")
        s_exp = sem("b_exp")
        s_pt = sem("b_pt")
        s_ptev = sem("b_ptev")
        s_pv = sem("b_pv")
        s_oh = sem("b_oh")
        s_ost = sem("b_ost")
        s_orow = sem("b_orow")
        s_ot = sem("b_ot")
        s_ohi = sem("b_ohi")
        s_olo = sem("b_olo")

        with nc.Block() as block:
            @block.sync
            def _(sp):
                sp.dma_start(ident[:, :], d["ident"]).then_inc(s_const, 16)
                sp.dma_start(hmask[:, :], d["head_mask"]).then_inc(s_const, 16)
                sp.dma_start(row_exp[:, :, :], d["row_exp"].rearrange("r (u c) -> r u c", u=2)).then_inc(s_const, 16)
                sp.dma_start(pages[:, :], d["page_table"].rearrange("b j -> (b j)").unsqueeze(0)).then_inc(s_pages, 16)
                for g in range(3):
                    sp.dma_start(cb[:, g, :, :], d["o_b"][g].rearrange("(i p) c -> p i c", p=P)).then_inc(s_cb, 16)
                sp.dma_start(q_row[:, :, :], d["z_qa"].rearrange("r c -> (r c)").rearrange("(u p e) -> p u e", u=2, e=HD)).then_inc(s_q, 16)
                new = d["z_a"][SEQ:T, :]
                sp.dma_start(k_new[:, :], new[:, 512:640]).then_inc(s_q, 16)
                sp.wait_ge(s_pad, 1)
                sp.dma_start(v_new[0:NS, :], new[:, 640:768]).then_inc(s_q, 16)
                sp.wait_ge(s_pages, 16)
                for q in range(PAGED * NPG, DB * NPG):
                    pg = sp.value_load(pages[0:1, q:q + 1], min_val=0, max_val=d["n_phys"] - 1)
                    b = q // NPG - PAGED
                    sp.dma_start(kv_late[:, b, q % NPG, :], d["cache_attn_kv"][bass.ds(pg, 1), :, :].rearrange("a p c -> (a p) c")).then_inc(s_kv[b], 16)
                os_rows = d["o_s"].rearrange("r c -> (r c)").rearrange("(u p e) -> u p e", u=2, e=HD)
                for u in range(2):
                    sp.wait_ge(s_oh, u + 1)
                    sp.dma_start(os_rows[u], o_half[:, u, 1, :]).then_inc(s_ost, 16)
                sp.wait_ge(s_ost, 32)
                sp.dma_start(o_row[:, :], d["o_s"]).then_inc(s_orow, 16)

            @block.scalar
            def _(act):
                act.wait_ge(s_diff, 1)
                act.activation(ex[:, :, :, :], ex[:, :, :, :], ACT.Exp).then_inc(s_ex, 1)
                act.wait_ge(s_qt, 1)
                act.activation(q_t[:, :, :], p_x[:, 0, 0:2 * P].rearrange("p (u c) -> p u c", u=2), ACT.Copy)
                act.activation(k_newt[:, :], p_x[:, 1, 0:NS], ACT.Copy).then_inc(s_qtev, 1)
                for b in range(DB):
                    act.wait_ge(s_kt, b + 1)
                    if b >= 2:
                        act.wait_ge(s_qk, b - 1)
                    act.activation(k_t[:, b % 2, :].rearrange("p (a c) -> p a c", a=2), p_x[:, :, :], ACT.Copy).then_inc(s_ktev, 1)
                    if b % 4 == 3:
                        u = b // 4
                        act.wait_ge(s_sm, u + 1)
                        act.activation(probs[:, 0:NKS], probs[:, 0:NKS], ACT.Exp, scale=-1.0, bias=st[:, u, 0:1],
                                       accum_out=st[:, u, 1:2]).then_inc(s_exp, 1)
                        for c in range(3):
                            w = min(4, 9 - 4 * c)
                            act.wait_ge(s_pt, 3 * u + c + 1)
                            act.activation(probs_t[:, 4 * c:4 * c + w, :], p_t[:, c % 2, 0:w * P].rearrange("p (a c) -> p a c", c=P),
                                           ACT.Copy).then_inc(s_ptev, 1)
                for i in range(NT):
                    act.wait_ge(s_ct, i + 1)
                    act.activation(ob[0][:, :, i * P:(i + 1) * P], p_t[:, i % 2, 0:256].rearrange("p (a c) -> p a c", a=2), ACT.Copy).then_inc(s_chi, 1)
                act.wait_ge(s_ot, 1)
                act.activation(oa[0][:, :, SEQ:T], p_n[:, 0:4 * NS].rearrange("p (a c) -> p a c", a=4), ACT.Copy).then_inc(s_ohi, 1)

            @block.gpsimd
            def _(pool):
                pool.memset(v_new[:, :], 0.0).then_inc(s_pad, 1)
                pool.memset(probs[:, NKS:9 * P], 0.0).then_inc(s_pad, 1)

            @block.vector
            def _(dve):
                own = [0]

                def chain(ins):
                    own[0] += 1
                    ins.then_inc(s_dv, 1)
                    dve.wait_ge(s_dv, own[0])

                dve.wait_ge(s_const, 48)
                dve.wait_ge(s_q, 48)
                for u in range(2):
                    for g in range(AKV):
                        q = dve.tensor_scalar(q_exp[:, u, g * HD:(g + 1) * HD], q_row[:, u, :], hmask[:, g:g + 1], None, ALU.mult)
                q.then_inc(s_qexp, 1)
                dve.wait_ge(s_cb, 48)
                nm = [cb[:, g, :, 256:260] for g in range(3)]
                chain(dve.tensor_tensor(low[:, :, 0, :], nm[0], nm[1], ALU.min))
                chain(dve.tensor_tensor(low[:, :, 1, :], low[:, :, 0, :], nm[2], ALU.min))
                for g in range(3):
                    t = dve.tensor_tensor(ex[:, g, :, :], low[:, :, 1, :], nm[g], ALU.subtract)
                t.then_inc(s_diff, 1)
                dve.wait_ge(s_ex, 1)
                for g in range(3):
                    t = dve.tensor_tensor(tot[:, g, :, :], ex[:, g, :, :], cb[:, g, :, 260:264], ALU.mult)
                chain(t)
                chain(dve.tensor_tensor(tot[:, 0, :, :], tot[:, 0, :, :], tot[:, 1, :, :], ALU.add))
                chain(dve.tensor_tensor(tot[:, 0, :, :], tot[:, 0, :, :], tot[:, 2, :, :], ALU.add))
                chain(dve.reciprocal(tot[:, 1, :, :], tot[:, 0, :, :]))
                for g in range(3):
                    t = dve.tensor_tensor(ex[:, g, :, :], ex[:, g, :, :], tot[:, 1, :, :], ALU.mult)
                chain(t)

                def soft(u):
                    dve.wait_ge(s_qk, 4 * u + 4)
                    if u:
                        dve.wait_ge(s_pt, 3)
                    dve.tensor_scalar(probs[:, 0:PAST].rearrange("p (a c) -> p a c", a=2), p_s[:, :, :], -ATT_SCALE, None, ALU.mult)
                    chain(dve.tensor_scalar(probs[:, PAST:NKS], p_n[:, 0:NS], -ATT_SCALE, None, ALU.mult))
                    dve.tensor_reduce(st[:, u, 0:1], probs[:, 0:NKS], AX, ALU.min).then_inc(s_sm, 1)

                def out(u):
                    dve.wait_ge(s_exp, u + 1)
                    chain(dve.reciprocal(st[:, u, 2:3], st[:, u, 1:2]))
                    chain(dve.tensor_scalar(st[:, u, 3:5], hmask[:, 0:2], st[:, u, 2:3], None, ALU.mult))
                    dve.wait_ge(s_pv, 4 * u + 4)
                    chain(dve.tensor_scalar(o_half[:, u, 0, :], p_o[:, 0:HD], st[:, u, 3:4], None, ALU.mult))
                    dve.scalar_tensor_tensor(out=o_half[:, u, 1, :], in0=p_o[:, HD:P], scalar=st[:, u, 4:5], in1=o_half[:, u, 0, :],
                                             op0=ALU.mult, op1=ALU.add).then_inc(s_oh, 1)

                def weighted(g, dst):
                    n = cb[:, g, :, 0:256].rearrange("p i (h e) -> p i h e", h=BH)
                    return [dve.tensor_tensor(dst[:, i, :].rearrange("p (h e) -> p h e", h=BH), n[:, i, :, :],
                                              ex[:, g, i, :].unsqueeze(2).broadcast_to([P, BH, HD]), ALU.mult) for i in range(NT)][-1]

                weighted(0, ob_row)
                chain(weighted(1, term))
                chain(dve.tensor_tensor(ob_row[:, :, :], ob_row[:, :, :], term[:, :, :], ALU.add))
                chain(weighted(2, term))
                dve.tensor_tensor(ob_row[:, :, :], ob_row[:, :, :], term[:, :, :], ALU.add).then_inc(s_obrow, 1)
                soft(0)
                out(0)
                soft(1)
                out(1)
                for i in range(NT):
                    dve.wait_ge(s_chi, i + 1)
                    dve.tensor_tensor(ob[1][:, :, i * P:(i + 1) * P], p_t[:, i % 2, 0:256].rearrange("p (a c) -> p a c", a=2),
                                      ob[0][:, :, i * P:(i + 1) * P].bitcast(F32), ALU.subtract).then_inc(s_clo, 1)
                dve.wait_ge(s_ohi, 1)
                dve.tensor_tensor(oa[1][:, :, SEQ:T], p_n[:, 0:4 * NS].rearrange("p (a c) -> p a c", a=4),
                                  oa[0][:, :, SEQ:T].bitcast(F32), ALU.subtract)

            @block.tensor
            def _(pe):
                pe.wait_ge(s_const, 48)
                pe.wait_ge(s_q, 48)
                pe.wait_ge(s_pad, 2)
                pe.wait_ge(s_qexp, 1)
                for u in range(2):
                    pe.transpose(p_x[:, 0, u * P:(u + 1) * P], q_exp[:, u, :], ident[:, :])
                pe.transpose(p_x[:, 1, 0:NS], k_new[:, :], ident[0:NS, 0:NS]).then_inc(s_qt, 1)

                def kv_of(b):
                    return kv_pages[:, b, :, :] if b < PAGED else kv_late[:, b - PAGED, :, :]

                def turn_keys(b):
                    if b >= PAGED:
                        pe.wait_ge(s_kv[b - PAGED], 16 * NPG)
                    if b:
                        pe.wait_ge(s_ktev, b)
                    else:
                        pe.wait_ge(s_qtev, 1)
                    for j in range(NPG):
                        t = pe.transpose(p_x[:, j // 4, j % 4 * P:(j % 4 + 1) * P], kv_of(b)[:, j, 0:P], ident[:, :])
                    t.then_inc(s_kt, 1)

                def values(u):
                    for c in range(3):
                        pe.wait_ge(s_exp, u + 1)
                        if c == 2:
                            pe.wait_ge(s_ptev, 3 * u + 1)
                        elif u:
                            pe.wait_ge(s_ptev, 3)
                        for k in range(4 * c, min(4 * c + 4, 9)):
                            t = pe.transpose(p_t[:, c % 2, k % 4 * P:(k % 4 + 1) * P], probs[:, k * P:(k + 1) * P], ident[:, :])
                        t.then_inc(s_pt, 1)
                    pe.wait_ge(s_ptev, 3 * u + 3)
                    if u:
                        pe.wait_ge(s_oh, u)
                    for b in range(4):
                        r = 32 * b
                        for k in range(9):
                            v = kv_of(4 * u + b)[:, k, P:2 * P] if k < NPG else v_new[:, :]
                            m = pe.matmul(p_o[r:r + 32, 0:P], probs_t[:, k, r:r + 32], v, start=(k == 0), stop=(k == 8))
                        m.then_inc(s_pv, 1)

                turn_keys(0)
                for b in range(DB):
                    u, r = b // 4, 32 * (b % 4)
                    if b % 4 == 0:
                        if u:
                            pe.wait_ge(s_sm, 1)
                        bias = sel[0:NS, SEL_OFF["s"]:SEL_OFF["s"] + NKS]
                        for c in range(2):
                            pe.matmul(p_s[:, c, :], row_exp[:, u, :], bias[:, 512 * c:512 * c + 512], start=True, stop=False, skip_group_check=True)
                        pe.matmul(p_n[:, 0:NS], row_exp[:, u, :], bias[:, PAST:NKS], start=True, stop=False, skip_group_check=True)
                        pe.wait_ge(s_qtev, 1)
                        pe.matmul(p_n[:, 0:NS], q_t[:, u, :], k_newt[:, :], start=False, stop=True, skip_group_check=True)
                    pe.wait_ge(s_ktev, b + 1)
                    for c in range(2):
                        m = pe.matmul(p_s[r:r + 32, c, :], q_t[:, u, r:r + 32], k_t[:, b % 2, 512 * c:512 * c + 512], start=False, stop=True,
                                      skip_group_check=True)
                    m.then_inc(s_qk, 1)
                    if b + 1 < DB and b % 4 != 3:
                        turn_keys(b + 1)
                    if b % 4 == 3:
                        if b + 1 < DB:
                            turn_keys(b + 1)
                        values(u)
                pe.wait_ge(s_obrow, 1)
                pe.wait_ge(s_ptev, 6)
                for i in range(NT):
                    if i >= 2:
                        pe.wait_ge(s_chi, i - 1)
                        pe.wait_ge(s_clo, i - 1)
                    for c in range(2):
                        t = pe.transpose(p_t[:, i % 2, c * P:(c + 1) * P], ob_row[:, i, c * P:(c + 1) * P], ident[:, :])
                    t.then_inc(s_ct, 1)
                pe.wait_ge(s_orow, 16)
                pe.wait_ge(s_sm, 2)
                for c in range(4):
                    t = pe.transpose(p_n[:, c * NS:(c + 1) * NS], o_row[:, c * P:(c + 1) * P], ident[0:NS, 0:NS])
                t.then_inc(s_ot, 1)


def attend_sample_b(nc, d, ob, m_in, w_raw):
    GW = (P, P, HD)
    KR = 6
    ctx = ExitStack()
    with ctx:
        sb, ps, sem = alloc(nc, ctx)
        ident = sb("ident4", [P, P])
        hmask = sb("hmask4", [P, AKV + BH])
        win = sb("win4", [P, 512])
        q_row = sb("q_row4", [P, 3, HD])
        q_exp = sb("q_exp4", [P, 3, BH, HD])
        q_t = sb("q_t4", [P, 3, 2, P])
        k_in = sb("k_in4", [P, KR, DS, 256])
        k_t = sb("k_t4", [P, 2, 1024])
        k_new = sb("k_new4", [NS, 3, 256])
        k_newt = sb("k_newt4", [P, 3, 2, NS])
        v1 = sb("v1", [P, DB, 1, 256])
        v2 = sb("v2", [P, DB, DS, 256])
        v3 = sb("v3", [P, DB, DS, 256])
        v_new = sb("v_new4", [P, 256])
        logit_t = sb("logit_t4", [P, 3, P])
        probs = sb("probs4", [P, 512])
        probs_t = sb("probs_t4", [P, 4, P])
        st = sb("st4", [P, 12, 3])
        p_x = ps("p_x4", [P, 2, 512])
        p_g = ps("p_g4", [P, 3, 512])
        p_r = ps("p_r4", [P, 3, 512])

        s_const = sem("c_const")
        s_q = sem("c_q")
        s_pad = sem("c_pad")
        s_k = [sem(f"c_k{u}") for u in range(KR)]
        s_v = sem("c_v")
        s_vpad = sem("c_vpad")
        s_mem = sem("c_mem")
        s_dv = sem("c_dv")
        s_qexp = sem("c_qexp")
        s_qt = sem("c_qt")
        s_qtev = sem("c_qtev")
        s_kt = sem("c_kt")
        s_ktA = sem("c_ktA")
        s_ktD = sem("c_ktD")
        s_g = sem("c_g")
        s_gev = sem("c_gev")
        s_r = sem("c_r")
        s_sm = sem("c_sm")
        s_e = sem("c_e")
        s_diff = sem("c_diff")
        s_w = sem("c_w")
        s_pn = sem("c_pn")
        s_pt = sem("c_pt")
        s_ptev = sem("c_ptev")
        s_pv = sem("c_pv")
        s_hi = sem("c_hi")

        units = [(g, b) for g in range(3) for b in range(DB)]

        def unit_rows(g, b):
            c = d["cache_win"][g][b]
            if g == 0:
                return c[0:P, :].unsqueeze(1)
            v = c.rearrange("(j r) c -> j r c", r=GROUPS[g][1])
            return v[:, 0:DS, :]
        nres = (1, DS, DS)
        turned = (p_x, p_r[:, 0:2, :])
        wide = [n for n, (g, b) in enumerate(units) if 2 * nres[g] * GW[g] > 512]
        vals = (v1, v2, v3)

        with nc.Block() as block:
            @block.sync
            def _(sp):
                sp.dma_start(ident[:, :], d["ident"]).then_inc(s_const, 16)
                sp.dma_start(hmask[:, :], d["head_mask"]).then_inc(s_const, 16)
                sp.dma_start(win[:, :], d["win_mask"]).then_inc(s_const, 16)
                sp.wait_ge(s_pad, 1)
                for g in range(3):
                    new = d["z_b"][g][SEQ:T, :]
                    sp.dma_start(q_row[:, g, :], d["z_qb"][g].rearrange("r c -> (r c)").rearrange("(p e) -> p e", e=HD)).then_inc(s_q, 16)
                    sp.dma_start(k_new[:, g, :], new[:, 256:512]).then_inc(s_q, 16)
                    sp.dma_start(v_new[NS * g:NS * g + NS, :], new[:, 512:768]).then_inc(s_q, 16)
                for n, (g, b) in enumerate(units):
                    if n >= KR:
                        sp.wait_ge(s_kt, n - KR + 1)
                    src = unit_rows(g, b)
                    r = src.shape[0]
                    sp.dma_start(k_in[0:r, n % KR, 0:nres[g], :], src[:, :, 0:256]).then_inc(s_k[n % KR], 16)
                sp.dma_start(m_in[:, :, :], d["mem_prompt"].rearrange("(i p) c -> p i c", p=P)).then_inc(s_mem, 16)
                sp.dma_start(w_raw[:, :, :], d["w_mem_kv"][0].rearrange("(k p) c -> p k c", p=P)).then_inc(s_mem, 16)
                sp.wait_ge(s_mem, 32)

            @block.gpsimd
            def _(pool):
                pool.memset(v_new[:, :], 0.0).then_inc(s_pad, 1)
                pool.memset(probs[:, :], 0.0).then_inc(s_pad, 1)
                for n, (g, b) in enumerate(units):
                    if n > 4:
                        pool.wait_ge(s_kt, n - 4)
                    if (g, b) == (2, 0):
                        pool.wait_ge(s_vpad, 1)
                    src = unit_rows(g, b)
                    pool.dma_start(vals[g][0:src.shape[0], b, :, :], src[:, :, 256:512]).then_inc(s_v, 16)

            @block.scalar
            def _(act):
                act.wait_ge(s_qt, 1)
                act.activation(q_t[:, 0:2, :, :].rearrange("p g c r -> p (g c) r"), p_x[:, 0, :].rearrange("p (g c) -> p g c", c=P), ACT.Copy)
                act.activation(q_t[:, 2, :, :], p_x[:, 1, 0:256].rearrange("p (g c) -> p g c", c=P), ACT.Copy)
                act.activation(k_newt[:, :, :, :].rearrange("p g c r -> p (g c r)"), p_x[:, 1, 256:256 + 6 * NS], ACT.Copy).then_inc(s_qtev, 1)
                for n, (g, b) in enumerate(units):
                    w = min(512, 2 * nres[g] * GW[g])
                    act.wait_ge(s_kt, n + 1)
                    if n >= 2:
                        act.wait_ge(s_g, n - 1)
                    act.activation(k_t[:, n % 2, 0:w], turned[n % 2][:, 0, 0:w], ACT.Copy).then_inc(s_ktA, 1)
                    if b == DB - 1:
                        act.wait_ge(s_g, n + 1)
                        act.activation(logit_t[0:GW[g], g, :], p_g[0:GW[g], g, 0:P], ACT.Copy).then_inc(s_gev, 1)
                act.wait_ge(s_sm, 1)
                for g in range(3):
                    c, w = P * g, GW[g]
                    act.activation(probs[:, c:c + w], probs[:, c:c + w], ACT.Exp, scale=-1.0, bias=st[:, 2, g:g + 1], accum_out=st[:, 3, g:g + 1])
                    c = 384 + NS * g
                    e = act.activation(probs[:, c:c + NS], probs[:, c:c + NS], ACT.Exp, scale=-1.0, bias=st[:, 2, g:g + 1], accum_out=st[:, 4, g:g + 1])
                e.then_inc(s_e, 1)
                act.wait_ge(s_diff, 1)
                act.activation(st[:, 6, :], st[:, 5, :], ACT.Exp).then_inc(s_w, 1)
                act.wait_ge(s_pt, 1)
                act.activation(probs_t[:, :, :], p_x[:, 0, :].rearrange("p (g c) -> p g c", c=P), ACT.Copy).then_inc(s_ptev, 1)
                act.wait_ge(s_pv, 1)
                for c in range(2):
                    for half in range(2):
                        r = HD * half
                        h = act.activation(ob[0][r:r + HD, c, SEQ:T], p_g[r:r + HD, c, 2 * c + half:P:BH], ACT.Copy)
                h.then_inc(s_hi, 1)

            @block.vector
            def _(dve):
                own = [0]

                def chain(ins):
                    own[0] += 1
                    ins.then_inc(s_dv, 1)
                    dve.wait_ge(s_dv, own[0])

                dve.memset(v3[:, :, :, :], 0.0).then_inc(s_vpad, 1)
                dve.wait_ge(s_const, 48)
                dve.wait_ge(s_q, 144)
                for h in range(BH):
                    q = dve.tensor_scalar(q_exp[:, :, h, :], q_row[:, :, :], hmask[:, AKV + h:AKV + h + 1], None, ALU.mult)
                q.then_inc(s_qexp, 1)
                for n in wide:
                    dve.wait_ge(s_kt, n + 1)
                    dve.wait_ge(s_g, n - 1)
                    dve.tensor_copy(k_t[:, n % 2, 512:1024], turned[n % 2][:, 1, :]).then_inc(s_ktD, 1)
                dve.wait_ge(s_r, 1)
                dve.wait_ge(s_pad, 2)
                for g in range(3):
                    c, w = P * g, GW[g]
                    src = p_r[:, 0, c:c + w] if g < 2 else p_r[:, 1, 0:w]
                    dve.tensor_tensor_reduce(out=probs[:, c:c + w], in0=src, in1=win[:, c:c + w], scale=-ATT_SCALE, scalar=3.0e38,
                                             op0=ALU.add, op1=ALU.min, accum_out=st[:, 0, g:g + 1])
                    c = 384 + NS * g
                    t = dve.tensor_tensor_reduce(out=probs[:, c:c + NS], in0=p_r[:, 2, NS * g:NS * g + NS], in1=win[:, c:c + NS], scale=-ATT_SCALE,
                                                 scalar=3.0e38, op0=ALU.add, op1=ALU.min, accum_out=st[:, 1, g:g + 1])
                chain(t)
                dve.tensor_tensor(st[:, 2, :], st[:, 0, :], st[:, 1, :], ALU.min).then_inc(s_sm, 1)
                dve.wait_ge(s_sm, 1)
                chain(dve.tensor_reduce(st[:, 7, 0:1], st[:, 2, :], AX, ALU.min))
                dve.tensor_tensor(st[:, 5, :], st[:, 7, 0:1].broadcast_to([P, 3]), st[:, 2, :], ALU.subtract).then_inc(s_diff, 1)
                dve.wait_ge(s_e, 1)
                chain(dve.tensor_tensor(st[:, 8, :], st[:, 3, :], st[:, 4, :], ALU.add))
                dve.wait_ge(s_w, 1)
                chain(dve.tensor_tensor(st[:, 9, :], st[:, 8, :], st[:, 6, :], ALU.mult))
                chain(dve.tensor_reduce(st[:, 7, 1:2], st[:, 9, :], AX, ALU.add))
                chain(dve.reciprocal(st[:, 7, 2:3], st[:, 7, 1:2]))
                chain(dve.tensor_scalar(st[:, 10, :], st[:, 6, :], st[:, 7, 2:3], None, ALU.mult))
                for g in range(3):
                    c, w = P * g, GW[g]
                    dve.tensor_scalar(probs[:, c:c + w], probs[:, c:c + w], st[:, 10, g:g + 1], None, ALU.mult)
                    c = 384 + NS * g
                    t = dve.tensor_scalar(probs[:, c:c + NS], probs[:, c:c + NS], st[:, 10, g:g + 1], None, ALU.mult)
                t.then_inc(s_pn, 1)
                dve.wait_ge(s_hi, 1)
                for c in range(2):
                    for half in range(2):
                        r = HD * half
                        dve.tensor_tensor(ob[1][r:r + HD, c, SEQ:T], p_g[r:r + HD, c, 2 * c + half:P:BH],
                                          ob[0][r:r + HD, c, SEQ:T].bitcast(F32), ALU.subtract)

            @block.tensor
            def _(pe):
                pe.wait_ge(s_const, 48)
                pe.wait_ge(s_q, 144)
                pe.wait_ge(s_qexp, 1)
                for g in range(3):
                    for c in range(2):
                        k = 2 * g + c
                        pe.transpose(p_x[:, k // 4, k % 4 * P:(k % 4 + 1) * P], q_exp[:, g, 2 * c:2 * c + 2, :].rearrange("p h e -> p (h e)"), ident[:, :])
                for g in range(3):
                    for c in range(2):
                        k = 256 + NS * (2 * g + c)
                        t = pe.transpose(p_x[:, 1, k:k + NS], k_new[:, g, c * P:(c + 1) * P], ident[0:NS, 0:NS])
                t.then_inc(s_qt, 1)

                def taken(n):
                    pe.wait_ge(s_ktA, n + 1)
                    if n in wide:
                        pe.wait_ge(s_ktD, wide.index(n) + 1)

                for n in range(len(units) + 1):
                    if n < len(units):
                        g, b = units[n]
                        pe.wait_ge(s_k[n % KR], 16 * (n // KR + 1))
                        if n == 0:
                            pe.wait_ge(s_qtev, 1)
                        if n >= 2:
                            taken(n - 2)
                        w = GW[g]
                        for t in range(nres[g]):
                            for c in range(2):
                                k = (2 * t + c) * w
                                m = pe.transpose(turned[n % 2][:, k // 512, k % 512:k % 512 + w], k_in[0:w, n % KR, t, c * P:(c + 1) * P], ident[0:w, 0:w])
                        m.then_inc(s_kt, 1)
                    if n:
                        g, b = units[n - 1]
                        w, reads = GW[g], DS * BH // nres[g]
                        taken(n - 1)
                        for t in range(nres[g]):
                            col = b * DS * BH + t * BH
                            for c in range(2):
                                k = (2 * t + c) * w
                                m = pe.matmul(p_g[0:w, g, col:col + reads], k_t[:, (n - 1) % 2, k:k + w], q_t[:, g, c, col:col + reads],
                                              start=(c == 0), stop=(c == 1))
                        m.then_inc(s_g, 1)
                for g in range(3):
                    for c in range(2):
                        pe.matmul(p_r[:, 2, NS * g:NS * g + NS], q_t[:, g, c, :], k_newt[:, g, c, :], start=(c == 0), stop=(c == 1))
                for g in range(3):
                    pe.wait_ge(s_gev, g + 1)
                    w = GW[g]
                    o = p_r[:, 0, P * g:P * g + w] if g < 2 else p_r[:, 1, 0:w]
                    t = pe.transpose(o, logit_t[0:w, g, :], ident[0:w, 0:w])
                t.then_inc(s_r, 1)
                pe.wait_ge(s_pn, 1)
                for k in range(4):
                    t = pe.transpose(p_x[:, 0, k * P:(k + 1) * P], probs[:, k * P:(k + 1) * P], ident[:, :])
                t.then_inc(s_pt, 1)
                pe.wait_ge(s_ptev, 1)
                pe.wait_ge(s_v, 16 * len(units))
                for c in range(2):
                    o = p_g[:, c, 0:P]
                    pe.matmul(o, v_new[:, c * P:(c + 1) * P], probs_t[:, 3, :], start=True, stop=False, skip_group_check=True)
                    for n, (g, b) in enumerate(units):
                        reads = DS * BH // nres[g]
                        for t in range(nres[g]):
                            col = b * DS * BH + t * BH
                            m = pe.matmul(o[:, col:col + reads], vals[g][:, b, t, c * P:(c + 1) * P], probs_t[:, g, col:col + reads],
                                          start=False, stop=True, skip_group_check=True)
                m.then_inc(s_pv, 1)


def mem_project(nc, d, km_t, vm, m_in, w_raw):
    ctx = ExitStack()
    with ctx:
        sb, ps, sem = alloc(nc, ctx)
        ident = sb("ident5", [P, P])
        m_hi = sb("m_hi", [P, KC, 2 * P], F32R)
        m_lo = sb("m_lo", [P, KC, 2 * P], F32R)
        w_hi = sb("w_hi5", [P, KC, 512], F32R)
        w_lo = sb("w_lo5", [P, KC, 512], F32R)
        k_row = sb("k_row5", [P, 2, 256])
        p_m = ps("p_m", [P, 4, 512])
        p_z = ps("p_z5", [P, 2, 512])
        p_k = ps("p_k5", [P, 512])
        s_in = sem("m_in_s")
        s_t = sem("m_t")
        s_hi = sem("m_hi_s")
        s_lo = sem("m_lo_s")
        s_whi = sem("m_whi")
        s_wlo = sem("m_wlo")
        s_z = sem("m_z")
        s_ev = sem("m_ev")
        s_kt = sem("m_kt")
        s_ktev = sem("m_ktev")
        s_out = sem("m_out")
        with nc.Block() as block:
            @block.sync
            def _(sp):
                sp.dma_start(ident[:, :], d["ident"]).then_inc(s_in, 16)
                for i in range(2):
                    sp.wait_ge(s_ev, 2 * i + 2)
                    sp.dma_start(d["new_mem_kv"][i * P:(i + 1) * P, 0:256], k_row[:, i, :]).then_inc(s_out, 16)
                    sp.dma_start(d["new_mem_kv"][i * P:(i + 1) * P, 256:512], vm[:, i, :]).then_inc(s_out, 16)
                sp.wait_ge(s_out, 64)

            @block.scalar
            def _(act):
                for u in range(2):
                    act.activation(w_hi[:, 4 * u:4 * u + 4, :], w_raw[:, 4 * u:4 * u + 4, :], ACT.Copy).then_inc(s_whi, 1)
                act.wait_ge(s_t, 1)
                for q in range(4):
                    a = act.activation(m_hi[:, 2 * q:2 * q + 2, :].rearrange("p k c -> p (k c)"), p_m[:, q, :], ACT.Copy)
                a.then_inc(s_hi, 1)
                for i in range(2):
                    act.wait_ge(s_z, i + 1)
                    act.activation(k_row[:, i, :], p_z[:, i, 0:256], ACT.Copy).then_inc(s_ev, 1)
                    act.activation(vm[:, i, :], p_z[:, i, 256:512], ACT.Copy).then_inc(s_ev, 1)
                act.wait_ge(s_kt, 1)
                act.activation(km_t[:, :, :].rearrange("p c k -> p (c k)"), p_k[:, :], ACT.Copy).then_inc(s_ktev, 1)

            @block.vector
            def _(dve):
                for u in range(2):
                    dve.wait_ge(s_whi, u + 1)
                    dve.tensor_tensor(w_lo[:, 4 * u:4 * u + 4, :], w_raw[:, 4 * u:4 * u + 4, :], w_hi[:, 4 * u:4 * u + 4, :].bitcast(F32), ALU.subtract).then_inc(s_wlo, 1)
                dve.wait_ge(s_hi, 1)
                for q in range(4):
                    a = dve.tensor_tensor(m_lo[:, 2 * q:2 * q + 2, :].rearrange("p k c -> p (k c)"), p_m[:, q, :],
                                          m_hi[:, 2 * q:2 * q + 2, :].rearrange("p k c -> p (k c)").bitcast(F32), ALU.subtract)
                a.then_inc(s_lo, 1)

            @block.tensor
            def _(pe):
                pe.wait_ge(s_in, 16)
                for k in range(KC):
                    for i in range(2):
                        t = pe.transpose(p_m[:, k // 2, (k % 2 * 2 + i) * P:(k % 2 * 2 + i + 1) * P], m_in[:, i, k * P:(k + 1) * P], ident[:, :])
                t.then_inc(s_t, 1)
                pe.wait_ge(s_lo, 1)
                pe.wait_ge(s_wlo, 2)
                for i in range(2):
                    for k in range(KC):
                        for p, (a, b) in enumerate(((m_hi, w_hi), (m_lo, w_hi), (m_hi, w_lo))):
                            m = pe.matmul(p_z[:, i, :], a[:, k, i * P:(i + 1) * P], b[:, k, :], start=(k == 0 and p == 0), stop=(k == KC - 1 and p == 2))
                    m.then_inc(s_z, 1)
                pe.wait_ge(s_ev, 4)
                for c in range(2):
                    for i in range(2):
                        t = pe.transpose(p_k[:, (2 * c + i) * P:(2 * c + i + 1) * P], k_row[:, i, c * P:(c + 1) * P], ident[:, :])
                t.then_inc(s_kt, 1)


class InverseRoot:

    def __init__(self, name, sem, acc, inv, p_sum, ones):
        self.acc, self.inv, self.p_sum, self.ones = acc, inv, p_sum, ones
        self.s_sum, self.s_mean, self.s_root, self.s_inv = (sem(f"{name}_{x}") for x in ("sum", "mn", "root", "inv"))

    def tensor(self, pe):
        for t in range(3):
            if t >= 2:
                pe.wait_ge(self.s_mean, t - 1)
            pe.matmul(self.p_sum[:, t % 2, 0:THIRD], self.ones[:, :], self.acc[:, t * THIRD:(t + 1) * THIRD], start=True, stop=True).then_inc(self.s_sum, 1)

    def vector(self, dve):
        for t in range(3):
            dve.wait_ge(self.s_sum, t + 1)
            dve.tensor_scalar(self.inv[:, t * THIRD:(t + 1) * THIRD], self.p_sum[:, t % 2, 0:THIRD], 1.0 / D, EPS, ALU.mult, ALU.add).then_inc(self.s_mean, 1)
        for t in range(3):
            dve.wait_ge(self.s_root, t + 1)
            dve.reciprocal(self.inv[:, t * THIRD:(t + 1) * THIRD], self.inv[:, t * THIRD:(t + 1) * THIRD]).then_inc(self.s_inv, 1)

    def scalar(self, act):
        for t in range(3):
            act.wait_ge(self.s_mean, t + 1)
            act.activation(self.inv[:, t * THIRD:(t + 1) * THIRD], self.inv[:, t * THIRD:(t + 1) * THIRD], ACT.Sqrt).then_inc(self.s_root, 1)


class NormedRows:

    def __init__(self, name, sem, h_t, gain, inv, n, tmp):
        self.h_t, self.gain, self.inv, self.n, self.tmp = h_t, gain, inv, n, tmp
        self.s_tmp, self.s_hi, self.s_lo = (sem(f"{name}_{x}") for x in ("tmpd", "hi", "lo"))

    def vector(self, dve, t):
        for k in range(KC + 1):
            j = t * KC + k
            if k < KC:
                if j >= 2:
                    dve.wait_ge(self.s_hi, j - 1)
                    dve.wait_ge(self.s_lo, j - 1)
                dve.scalar_tensor_tensor(out=self.tmp[:, j % 2, :], in0=self.h_t[:, k, t * THIRD:(t + 1) * THIRD], scalar=self.gain[:, k:k + 1],
                                         in1=self.inv[:, t * THIRD:(t + 1) * THIRD], op0=ALU.mult, op1=ALU.mult).then_inc(self.s_tmp, 1)
            if k:
                j -= 1
                dve.wait_ge(self.s_hi, j + 1)
                dve.tensor_tensor(self.n[1][:, k - 1, t * THIRD:(t + 1) * THIRD], self.tmp[:, j % 2, :],
                                  self.n[0][:, k - 1, t * THIRD:(t + 1) * THIRD].bitcast(F32), ALU.subtract).then_inc(self.s_lo, 1)

    def scalar(self, act, t):
        for k in range(KC):
            j = t * KC + k
            act.wait_ge(self.s_tmp, j + 1)
            act.activation(self.n[0][:, k, t * THIRD:(t + 1) * THIRD], self.tmp[:, j % 2, :], ACT.Copy).then_inc(self.s_hi, 1)


def merge(nc, d, oa, ob, h_t, n, inv):
    ctx = ExitStack()
    with ctx:
        sb, ps, sem = alloc(nc, ctx)
        ident = sb("ident6", [P, P])
        ones = sb("ones6", [P, P])
        w_raw = sb("w_raw6", [P, 2, KC, P])
        w_hi = sb("w_hi6", [P, 2, KC, P], F32R)
        w_lo = sb("w_lo6", [P, 2, KC, P], F32R)
        gate = sb("gate6", [P, 3, 2, THIRD])
        x_in = gate[:, :, :, :].rearrange("p a b c -> p (a b c)")[:, 0:2 * D].rearrange("p (u c) -> p u c", u=2)
        prod = sb("prod6", [P, 2, 2, THIRD])
        acc = sb("acc6", [P, T])
        sq = sb("sq6", [P, 3, THIRD])
        p_y = ps("p_y6", [P, 2, 2, 512])
        p_x = ps("p_x6", [P, 2, 512])
        s_const = sem("e_const")
        s_x = [sem(f"e_x{u}") for u in range(2)]
        s_xt = sem("e_xt")
        s_xa = sem("e_xa")
        s_xd = sem("e_xd")
        s_w = [sem(f"e_w{u}") for u in range(2)]
        s_whi = sem("e_whi")
        s_wlo = sem("e_wlo")
        s_gate = [sem(f"e_gate{u}") for u in range(3)]
        s_y = sem("e_y")
        s_used = sem("e_used")
        s_ga = sem("e_ga")
        s_gb = sem("e_gb")
        s_ysum = sem("e_ysum")
        s_yhi = sem("e_yhi")
        s_ylo = sem("e_ylo")
        s_h = sem("e_h")
        s_sq = sem("e_sq")
        s_acc = sem("e_acc")
        root = InverseRoot("e_n", sem, acc, inv, p_x, ones)

        steps = [(m, t) for m in range(2 * KC) for t in range(3)]
        NBR = 3 * KC
        with nc.Block() as block:
            @block.sync
            def _(sp):
                sp.dma_start(ident[:, :], d["ident"]).then_inc(s_const, 16)
                sp.dma_start(ones[:, :], d["ones"]).then_inc(s_const, 16)

                def load_w(m):
                    if m >= 2:
                        sp.wait_ge(s_whi, m - 1)
                        sp.wait_ge(s_wlo, m - 1)
                    if m < KC:
                        cols = slice(m * P, (m + 1) * P)
                        sp.dma_start(w_raw[:, m % 2, 0:4, :], d["w_br_a"][0, :, cols].rearrange("(k p) c -> p k c", p=P)).then_inc(s_w[m % 2], 16)
                        sp.dma_start(w_raw[:, m % 2, 4:6, :], d["w_br_b"][0, :, cols].rearrange("(k p) c -> p k c", p=P)).then_inc(s_w[m % 2], 16)
                    else:
                        cols = slice((m - KC) * P, (m - KC + 1) * P)
                        sp.dma_start(w_raw[:, m % 2, :, :], d["w_out"][0, :, cols].rearrange("(k p) c -> p k c", p=P)).then_inc(s_w[m % 2], 32)

                def load_gate(s):
                    m, t = steps[s]
                    if s >= 3:
                        sp.wait_ge(s_gb, s - 2)
                    src = d["gates"].rearrange("(u f) t -> f u t", u=2)[m * P:(m + 1) * P, :, t * THIRD:(t + 1) * THIRD]
                    sp.dma_start(gate[:, s % 3, :, :], src).then_inc(s_gate[s % 3], 16)

                load_w(0)
                for i in range(TILES):
                    r0, r = i * P, (NS if i == NT else P)
                    if i >= 2:
                        sp.wait_ge(s_xt, i - 1)
                    sp.dma_start(x_in[0:r, i % 2, :], d["x_sample"] if i == NT else d["x_prompt"][r0:r0 + r, :]).then_inc(s_x[i % 2], 16)
                load_w(1)
                sp.wait_ge(s_xt, TILES)
                for s in range(NBR):
                    load_gate(s)
                    if s % 3 == 1 and s // 3 + 2 < 2 * KC:
                        load_w(s // 3 + 2)
                for m in range(KC + 2, 2 * KC):
                    load_w(m)

            @block.scalar
            def _(act):
                def split_hi(m):
                    act.wait_ge(s_w[m % 2], 32 * (m // 2 + 1))
                    if m >= 2:
                        act.wait_ge(s_y, 3 * (m - 1))
                    k = 6 if m < KC else KC
                    act.activation(w_hi[:, m % 2, 0:k, :], w_raw[:, m % 2, 0:k, :], ACT.Copy).then_inc(s_whi, 1)

                split_hi(0)
                for i in range(TILES):
                    r = NS if i == NT else P
                    act.wait_ge(s_xt, i + 1)
                    act.activation(h_t[:, 0:4, i * P:i * P + r], p_x[:, 0, :].rearrange("p (k c) -> p k c", c=P)[:, :, 0:r], ACT.Copy).then_inc(s_xa, 1)
                split_hi(1)
                for s, (m, t) in enumerate(steps):
                    if m < KC:
                        act.wait_ge(s_ysum, s + 1)
                        act.activation(n[0][:, m, t * THIRD:(t + 1) * THIRD], prod[:, s % 2, 0, :], ACT.Copy).then_inc(s_yhi, 1)
                    else:
                        q = s - NBR
                        act.wait_ge(s_h, q + 1)
                        h = h_t[:, m - KC, t * THIRD:(t + 1) * THIRD]
                        if m == KC:
                            act.activation(acc[:, t * THIRD:(t + 1) * THIRD], h, ACT.Square).then_inc(s_sq, 1)
                        else:
                            if q >= 6:
                                act.wait_ge(s_acc, q - 5)
                            act.activation(sq[:, t, :], h, ACT.Square).then_inc(s_sq, 1)
                    if t == 2 and m + 2 < 2 * KC:
                        split_hi(m + 2)
                root.scalar(act)

            @block.gpsimd
            def _(pool):
                for q in range(3, NBR):
                    t = q % 3
                    pool.wait_ge(s_sq, q + 1)
                    if q >= 6:
                        pool.wait_ge(s_acc, q - 5)
                    a = acc[:, t * THIRD:(t + 1) * THIRD]
                    pool.tensor_tensor(a, a, sq[:, t, :], ALU.add).then_inc(s_acc, 1)

            @block.vector
            def _(dve):
                def split_lo(m):
                    dve.wait_ge(s_whi, m + 1)
                    k = 6 if m < KC else KC
                    dve.tensor_tensor(w_lo[:, m % 2, 0:k, :], w_raw[:, m % 2, 0:k, :], w_hi[:, m % 2, 0:k, :].bitcast(F32), ALU.subtract).then_inc(s_wlo, 1)

                def y_low(s):
                    m, t = steps[s]
                    dve.wait_ge(s_yhi, s + 1)
                    dve.tensor_tensor(n[1][:, m, t * THIRD:(t + 1) * THIRD], prod[:, s % 2, 0, :],
                                      n[0][:, m, t * THIRD:(t + 1) * THIRD].bitcast(F32), ALU.subtract).then_inc(s_ylo, 1)

                split_lo(0)
                for i in range(TILES):
                    r = NS if i == NT else P
                    dve.wait_ge(s_xt, i + 1)
                    dve.tensor_copy(h_t[:, 4:8, i * P:i * P + r], p_x[:, 1, :].rearrange("p (k c) -> p k c", c=P)[:, :, 0:r]).then_inc(s_xd, 1)
                split_lo(1)
                for s, (m, t) in enumerate(steps):
                    if m < KC:
                        dve.wait_ge(s_gate[s % 3], 16 * (s // 3 + 1))
                        dve.wait_ge(s_y, s + 1)
                        if s >= 2:
                            dve.wait_ge(s_ylo, s - 1)
                        dve.tensor_tensor(prod[:, s % 2, 0, :], p_y[:, s % 2, 0, 0:THIRD], gate[:, s % 3, 0, :], ALU.mult).then_inc(s_ga, 1)
                        dve.tensor_tensor(prod[:, s % 2, 1, :], p_y[:, s % 2, 1, 0:THIRD], gate[:, s % 3, 1, :], ALU.mult).then_inc(s_gb, 1)
                        if s:
                            y_low(s - 1)
                        dve.wait_ge(s_gb, s + 1)
                        dve.tensor_tensor(prod[:, s % 2, 0, :], prod[:, s % 2, 0, :], prod[:, s % 2, 1, :], ALU.add).then_inc(s_ysum, 1)
                        if s == NBR - 1:
                            y_low(s)
                    else:
                        h = h_t[:, m - KC, t * THIRD:(t + 1) * THIRD]
                        dve.wait_ge(s_y, s + 1)
                        dve.tensor_tensor(h, h, p_y[:, s % 2, 0, 0:THIRD], ALU.add).then_inc(s_h, 1)
                    if t == 2 and m + 2 < 2 * KC:
                        split_lo(m + 2)
                root.vector(dve)

            @block.tensor
            def _(pe):
                pe.wait_ge(s_const, 32)
                for i in range(TILES):
                    r = NS if i == NT else P
                    pe.wait_ge(s_x[i % 2], 16 * (i // 2 + 1))
                    if i:
                        pe.wait_ge(s_xa, i)
                        pe.wait_ge(s_xd, i)
                    for k in range(KC):
                        x = pe.transpose(p_x[:, k // 4, k % 4 * P:k % 4 * P + r], x_in[0:r, i % 2, k * P:(k + 1) * P], ident[0:r, 0:r])
                    x.then_inc(s_xt, 1)
                for s, (m, t) in enumerate(steps):
                    u = m % 2
                    if t == 0:
                        pe.wait_ge(s_whi, m + 1)
                        pe.wait_ge(s_wlo, m + 1)
                    if 2 <= s < NBR + 2:
                        pe.wait_ge(s_gb, min(s - 1, NBR))
                    if s >= NBR + 2:
                        pe.wait_ge(s_h, s - NBR - 1)
                    if m == KC:
                        pe.wait_ge(s_ylo, NBR)
                    c = slice(t * THIRD, (t + 1) * THIRD)
                    parts = [(oa, 0, 4, 0), (ob, 4, 6, 1)] if m < KC else [(n, 0, KC, 0)]
                    for src, k0, k1, bank in parts:
                        for k in range(k0, k1):
                            for p, (w, x) in enumerate(((w_hi, src[0]), (w_hi, src[1]), (w_lo, src[0]))):
                                y = pe.matmul(p_y[:, s % 2, bank, 0:THIRD], w[:, u, k, :], x[:, k - k0, c], start=(k == k0 and p == 0),
                                              stop=(k == k1 - 1 and p == 2))
                    y.then_inc(s_y, 1)
                pe.wait_ge(s_sq, 3)
                pe.wait_ge(s_acc, NBR - 3)
                root.tensor(pe)


def attend_mem(nc, d, km_t, vm, h_t, n, inv_in, inv_out):
    ctx = ExitStack()
    with ctx:
        sb, ps, sem = alloc(nc, ctx)
        ident = sb("ident7", [P, P])
        ones = sb("ones7", [P, P])
        gain = sb("gain7", [P, KC])
        w_raw = sb("w_raw7", [P, 2 * D])
        w_hi = sb("w_hi7", [P, 2 * D], F32R)
        w_lo = sb("w_lo7", [P, 2 * D], F32R)
        qm_t = sb("qm_t", [P, 2, T])
        om = [sb(f"om_{x}", [P, 2, T], F32R) for x in ("hi", "lo")]
        probs = sb("probs7", [P, 2, D])
        probs_t = sb("probs_t7", [P, 2, D])
        om_row = sb("om_row", [P, 2, 256])
        top = sb("top7", [P, 2, BH])
        den = sb("den7", [P, 4, BH])
        rden = sb("rden7", [P, 2, BH])
        k_in = sb("k_in7", [P, 2, 2, 256])
        v_s = sb("v_s7", [P, DB, 2, 256])
        k_t = sb("k_t7", [P, 2, 512])
        q_bd = sb("q_bd7", [P, 2, P])
        logit_t = sb("logit_t7", [P, 2, P])
        probs_s = sb("probs_s7", [P, 256])
        probs_st = sb("probs_st7", [P, 2, P])
        st = sb("st7", [P, 4])
        acc = probs[:, :, :].rearrange("p a b -> p (a b)")[:, 0:T]
        sq = probs_t[:, :, :].rearrange("p a b -> p (a b)")[:, 0:T].rearrange("p (a c) -> p a c", a=3)
        p_s = ps("p_s7", [P, 4, 512])
        p_t = ps("p_t7", [P, 2, 512])
        p_o = ps("p_o7", [P, 512])
        p_x = ps("p_x7", [P, 512])

        s_const = sem("f_const")
        s_w = [sem(f"f_w{u}") for u in range(2)]
        s_whi = sem("f_whi")
        s_wlo = sem("f_wlo")
        s_q = sem("f_q")
        s_qev = sem("f_qev")
        s_pad = sem("f_pad")
        s_bd = sem("f_bd")
        s_k = [sem(f"f_k{u}") for u in range(2)]
        s_v = sem("f_v")
        s_kt = sem("f_kt")
        s_ktev = sem("f_ktev")
        s_g = sem("f_g")
        s_gev = sem("f_gev")
        s_r = sem("f_r")
        s_smax = sem("f_smax")
        s_snm = sem("f_snm")
        s_se = sem("f_se")
        s_srd = sem("f_srd")
        s_spn = sem("f_spn")
        s_spt = sem("f_spt")
        s_sptev = sem("f_sptev")
        s_spv = sem("f_spv")
        s_shi = sem("f_shi")
        s_slo = sem("f_slo")
        s_qk = sem("f_qk")
        s_max = sem("f_max")
        s_nm = sem("f_nm")
        s_exp = sem("f_exp")
        s_pt = sem("f_pt")
        s_ptA = sem("f_ptA")
        s_ptD = sem("f_ptD")
        s_pv = sem("f_pv")
        s_rd = sem("f_rd")
        s_row = sem("f_row")
        s_ot = sem("f_ot")
        s_ohi = sem("f_ohi")
        s_olo = sem("f_olo")
        s_y = sem("f_y")
        s_h = sem("f_h")
        s_sq = sem("f_sq")
        s_acc = sem("f_acc")
        root = InverseRoot("f_n", sem, acc, inv_out, p_t, ones)
        normed = NormedRows("f_r", sem, h_t, gain, inv_in, n, sb("tmp7", [P, 2, THIRD]))

        NQ = 6
        outs = [(m, t) for m in range(KC) for t in range(3)]
        LAST = NT + 4
        with nc.Block() as block:
            @block.sync
            def _(sp):
                wq = d["w_mem_q"][0].rearrange("(k p) c -> p k c", p=P)
                for u in range(2):
                    sp.dma_start(w_raw[:, D * u:D * u + D].rearrange("p (k c) -> p k c", k=4), wq[:, 4 * u:4 * u + 4, :]).then_inc(s_w[u], 16)
                sp.dma_start(ident[:, :], d["ident"]).then_inc(s_const, 16)
                sp.dma_start(ones[:, :], d["ones"]).then_inc(s_const, 16)
                sp.dma_start(gain[:, :], d["g_mem"][0].rearrange("(k p) -> p k", p=P), allow_slow_non_contiguous=True).then_inc(s_const, 16)
                for b in range(DB):
                    if b >= 2:
                        sp.wait_ge(s_kt, b - 1)
                    src = d["cache_mem_kv"][b].rearrange("(a p) c -> p a c", p=P)
                    sp.dma_start(k_in[:, b % 2, :, :], src[:, :, 0:256]).then_inc(s_k[b % 2], 16)
                    sp.dma_start(v_s[:, b, :, :], src[:, :, 256:512]).then_inc(s_v, 16)
                sp.wait_ge(s_wlo, 2)
                for u in range(2):
                    sp.dma_start(w_raw[:, D * u:D * u + D], d["w_mem_o"][0, u * P:(u + 1) * P, :]).then_inc(s_w[u], 16)

            @block.scalar
            def _(act):
                def split_hi(f):
                    u = f % 2
                    act.wait_ge(s_w[u], 16 * (f // 2 + 1))
                    if f >= 2:
                        act.wait_ge(s_q, NQ)
                    act.activation(w_hi[:, D * u:D * u + D], w_raw[:, D * u:D * u + D], ACT.Copy).then_inc(s_whi, 1)

                split_hi(0)
                split_hi(1)
                for t in range(3):
                    normed.scalar(act, t)
                for s in range(NQ):
                    t, c = s // 2, s % 2
                    act.wait_ge(s_q, s + 1)
                    act.activation(qm_t[:, c, t * THIRD:(t + 1) * THIRD], p_s[:, s % 4, 0:THIRD], ACT.Copy).then_inc(s_qev, 1)
                for b in range(DB):
                    act.wait_ge(s_kt, b + 1)
                    if b >= 2:
                        act.wait_ge(s_g, b - 1)
                    act.activation(k_t[:, b % 2, :], p_t[:, b % 2, :], ACT.Copy).then_inc(s_ktev, 1)
                act.wait_ge(s_g, DB)
                act.activation(logit_t[:, :, :], p_x[:, 0:256].rearrange("p (a c) -> p a c", a=2), ACT.Copy).then_inc(s_gev, 1)
                act.wait_ge(s_snm, 1)
                act.activation(probs_s[:, :], p_x[:, 256:512], ACT.Exp, scale=ATT_SCALE, bias=st[:, 1:2], accum_out=st[:, 2:3]).then_inc(s_se, 1)
                for it in range(LAST):
                    i = it - 1
                    if 0 <= i < NT:
                        act.wait_ge(s_nm, i + 1)
                        if i >= 2:
                            act.wait_ge(s_pt, i - 1)
                        for h in range(BH):
                            e = act.activation(probs[:, i % 2, h * 256:(h + 1) * 256], p_s[:, i % 2 * 2 + h % 2, h // 2 * 256:h // 2 * 256 + 256], ACT.Exp,
                                               scale=ATT_SCALE, bias=top[:, i % 2, h:h + 1], accum_out=den[:, i % 4, h:h + 1])
                        e.then_inc(s_exp, 1)
                    i = it - 2
                    if 0 <= i < NT:
                        act.wait_ge(s_pt, i + 1)
                        if i >= 2:
                            act.wait_ge(s_pv, i - 1)
                        act.activation(probs_t[:, i % 2, 0:512], p_t[:, 0, :], ACT.Copy).then_inc(s_ptA, 1)
                    i = it - 3
                    if 0 <= i < NT:
                        act.wait_ge(s_ot, i + 1)
                        act.activation(om[0][:, :, i * P:(i + 1) * P], p_x[:, 0:256].rearrange("p (a c) -> p a c", a=2), ACT.Copy).then_inc(s_ohi, 1)
                split_hi(2)
                split_hi(3)
                act.wait_ge(s_spt, 1)
                act.activation(probs_st[:, :, :], p_x[:, 0:256].rearrange("p (a c) -> p a c", a=2), ACT.Copy).then_inc(s_sptev, 1)
                act.wait_ge(s_spv, 1)
                for c in range(2):
                    for half in range(2):
                        r = HD * half
                        e = act.activation(om[0][r:r + HD, c, SEQ:T], p_o[r:r + HD, c * P + 2 * c + half:(c + 1) * P:BH], ACT.Copy)
                e.then_inc(s_shi, 1)
                for s, (m, t) in enumerate(outs):
                    act.wait_ge(s_h, s + 1)
                    h = h_t[:, m, t * THIRD:(t + 1) * THIRD]
                    if m == 0:
                        act.activation(acc[:, t * THIRD:(t + 1) * THIRD], h, ACT.Square).then_inc(s_sq, 1)
                    else:
                        if m >= 2:
                            act.wait_ge(s_acc, s - 5)
                        act.activation(sq[:, t, :], h, ACT.Square).then_inc(s_sq, 1)
                root.scalar(act)

            @block.gpsimd
            def _(pool):
                pool.memset(q_bd[:, :, :], 0.0).then_inc(s_pad, 1)
                for s in range(3, len(outs)):
                    t = s % 3
                    pool.wait_ge(s_sq, s + 1)
                    if s >= 6:
                        pool.wait_ge(s_acc, s - 5)
                    a = acc[:, t * THIRD:(t + 1) * THIRD]
                    pool.tensor_tensor(a, a, sq[:, t, :], ALU.add).then_inc(s_acc, 1)

            @block.vector
            def _(dve):
                def split_lo(f):
                    u = f % 2
                    dve.wait_ge(s_whi, f + 1)
                    dve.tensor_tensor(w_lo[:, D * u:D * u + D], w_raw[:, D * u:D * u + D], w_hi[:, D * u:D * u + D].bitcast(F32), ALU.subtract).then_inc(s_wlo, 1)

                split_lo(0)
                split_lo(1)
                dve.wait_ge(s_const, 48)
                for t in range(3):
                    normed.vector(dve, t)
                dve.wait_ge(s_pad, 1)
                dve.wait_ge(s_qev, NQ)
                for c in range(2):
                    for half in range(2):
                        r = HD * half
                        e = dve.tensor_copy(q_bd[r:r + HD, c, 2 * c + half:P:BH], qm_t[r:r + HD, c, SEQ:T])
                e.then_inc(s_bd, 1)
                dve.wait_ge(s_r, 1)
                dve.tensor_reduce(st[:, 0:1], p_x[:, 256:512], AX, ALU.max).then_inc(s_smax, 1)
                dve.wait_ge(s_smax, 1)
                dve.tensor_scalar(st[:, 1:2], st[:, 0:1], -ATT_SCALE, None, ALU.mult).then_inc(s_snm, 1)
                dve.wait_ge(s_se, 1)
                dve.reciprocal(st[:, 3:4], st[:, 2:3]).then_inc(s_srd, 1)
                dve.wait_ge(s_srd, 1)
                dve.tensor_scalar(probs_s[:, :], probs_s[:, :], st[:, 3:4], None, ALU.mult).then_inc(s_spn, 1)
                for it in range(LAST):
                    i = it
                    if i < NT:
                        dve.wait_ge(s_qk, i + 1)
                        if i >= 2:
                            dve.wait_ge(s_exp, i - 1)
                        dve.tensor_reduce(rden[:, i % 2, :].rearrange("p (a c) -> p c a", a=2),
                                          p_s[:, i % 2 * 2:i % 2 * 2 + 2, :].rearrange("p a (c k) -> p a c k", c=2), AX, ALU.max).then_inc(s_max, 1)
                        dve.wait_ge(s_max, i + 1)
                        dve.tensor_scalar(top[:, i % 2, :], rden[:, i % 2, :], -ATT_SCALE, None, ALU.mult).then_inc(s_nm, 1)
                    i = it - 2
                    if 0 <= i < NT:
                        dve.wait_ge(s_pt, i + 1)
                        if i >= 2:
                            dve.wait_ge(s_pv, i - 1)
                        dve.tensor_copy(probs_t[:, i % 2, 512:1024], p_t[:, 1, :]).then_inc(s_ptD, 1)
                    i = it - 3
                    if 0 <= i < NT:
                        dve.wait_ge(s_pv, i + 1)
                        dve.reciprocal(den[:, i % 4, :], den[:, i % 4, :]).then_inc(s_rd, 1)
                        dve.wait_ge(s_rd, i + 1)
                        if i >= 2:
                            dve.wait_ge(s_ot, i - 1)
                        dve.tensor_tensor(om_row[:, i % 2, :].rearrange("p (h e) -> p h e", h=BH), p_o[:, 0:256].rearrange("p (h e) -> p h e", h=BH),
                                          den[:, i % 4, :].unsqueeze(2).broadcast_to([P, BH, HD]), ALU.mult).then_inc(s_row, 1)
                        dve.wait_ge(s_ohi, i + 1)
                        dve.tensor_tensor(om[1][:, :, i * P:(i + 1) * P], p_x[:, 0:256].rearrange("p (a c) -> p a c", a=2),
                                          om[0][:, :, i * P:(i + 1) * P].bitcast(F32), ALU.subtract).then_inc(s_olo, 1)
                split_lo(2)
                split_lo(3)
                dve.wait_ge(s_shi, 1)
                for c in range(2):
                    for half in range(2):
                        r = HD * half
                        e = dve.tensor_tensor(om[1][r:r + HD, c, SEQ:T], p_o[r:r + HD, c * P + 2 * c + half:(c + 1) * P:BH],
                                              om[0][r:r + HD, c, SEQ:T].bitcast(F32), ALU.subtract)
                e.then_inc(s_slo, 1)
                for s, (m, t) in enumerate(outs):
                    h = h_t[:, m, t * THIRD:(t + 1) * THIRD]
                    dve.wait_ge(s_y, s + 1)
                    dve.tensor_tensor(h, h, p_s[:, s % 4, 0:THIRD], ALU.add).then_inc(s_h, 1)
                root.vector(dve)

            @block.tensor
            def _(pe):
                pe.wait_ge(s_whi, 2)
                pe.wait_ge(s_wlo, 2)
                for s in range(NQ):
                    t, c = s // 2, s % 2
                    if s >= 4:
                        pe.wait_ge(s_qev, s - 3)
                    pe.wait_ge(normed.s_lo, KC * (t + 1))
                    for k in range(KC):
                        w = slice(k * 256 + c * P, k * 256 + (c + 1) * P)
                        x = slice(t * THIRD, (t + 1) * THIRD)
                        for p, (a, b) in enumerate(((w_hi, n[0]), (w_hi, n[1]), (w_lo, n[0]))):
                            m = pe.matmul(p_s[:, s % 4, 0:THIRD], a[:, w], b[:, k, x], start=(k == 0 and p == 0), stop=(k == KC - 1 and p == 2))
                    m.then_inc(s_q, 1)
                pe.wait_ge(s_const, 48)
                for b in range(DB + 1):
                    if b < DB:
                        pe.wait_ge(s_k[b % 2], 16 * (b // 2 + 1))
                        if b >= 2:
                            pe.wait_ge(s_ktev, b - 1)
                        for a in range(2):
                            for c in range(2):
                                x = pe.transpose(p_t[:, b % 2, (2 * a + c) * P:(2 * a + c + 1) * P], k_in[:, b % 2, a, c * P:(c + 1) * P], ident[:, :])
                        x.then_inc(s_kt, 1)
                    if b:
                        if b == 1:
                            pe.wait_ge(s_bd, 1)
                        pe.wait_ge(s_ktev, b)
                        q = slice(16 * (b - 1), 16 * b)
                        for a in range(2):
                            for c in range(2):
                                x = pe.matmul(p_x[:, a * P + 16 * (b - 1):a * P + 16 * b], k_t[:, (b - 1) % 2, (2 * a + c) * P:(2 * a + c + 1) * P],
                                              q_bd[:, c, q], start=(c == 0), stop=(c == 1))
                        x.then_inc(s_g, 1)
                pe.wait_ge(s_gev, 1)
                for a in range(2):
                    x = pe.transpose(p_x[:, 256 + a * P:256 + (a + 1) * P], logit_t[:, a, :], ident[:, :])
                x.then_inc(s_r, 1)
                pe.wait_ge(s_qev, NQ)
                for it in range(LAST):
                    i = it
                    if i < NT:
                        if i >= 2:
                            pe.wait_ge(s_exp, i - 1)
                        for h in range(BH):
                            lo = h % 2 * HD
                            m = pe.matmul(p_s[:, i % 2 * 2 + h % 2, h // 2 * 256:h // 2 * 256 + 256], qm_t[lo:lo + HD, h // 2, i * P:(i + 1) * P],
                                          km_t[lo:lo + HD, h // 2, :], start=True, stop=True)
                        m.then_inc(s_qk, 1)
                    i = it - 3
                    if 0 <= i < NT:
                        pe.wait_ge(s_row, i + 1)
                        if i:
                            pe.wait_ge(s_olo, i)
                        else:
                            pe.wait_ge(s_se, 1)
                        for c in range(2):
                            m = pe.transpose(p_x[:, c * P:(c + 1) * P], om_row[:, i % 2, c * P:(c + 1) * P], ident[:, :])
                        m.then_inc(s_ot, 1)
                    i = it - 1
                    if 0 <= i < NT:
                        pe.wait_ge(s_exp, i + 1)
                        if i:
                            pe.wait_ge(s_ptA, i)
                            pe.wait_ge(s_ptD, i)
                        for c in range(8):
                            m = pe.transpose(p_t[:, c // 4, c % 4 * P:(c % 4 + 1) * P], probs[:, i % 2, c * P:(c + 1) * P], ident[:, :])
                        m.then_inc(s_pt, 1)
                    i = it - 2
                    if 0 <= i < NT:
                        pe.wait_ge(s_ptA, i + 1)
                        pe.wait_ge(s_ptD, i + 1)
                        if i:
                            pe.wait_ge(s_row, i)
                        for h in range(BH):
                            for a in range(2):
                                m = pe.matmul(p_o[:, h * HD:(h + 1) * HD], probs_t[:, i % 2, h * 256 + a * P:h * 256 + (a + 1) * P],
                                              vm[:, a, h * HD:(h + 1) * HD], start=(a == 0), stop=(a == 1))
                        m.then_inc(s_pv, 1)
                pe.wait_ge(s_spn, 1)
                pe.wait_ge(s_olo, NT)
                for a in range(2):
                    x = pe.transpose(p_x[:, a * P:(a + 1) * P], probs_s[:, a * P:(a + 1) * P], ident[:, :])
                x.then_inc(s_spt, 1)
                pe.wait_ge(s_sptev, 1)
                pe.wait_ge(s_v, 16 * DB)
                pe.wait_ge(s_row, NT)
                for b in range(DB):
                    for c in range(2):
                        for a in range(2):
                            x = pe.matmul(p_o[:, c * P + 16 * b:c * P + 16 * b + 16], v_s[:, b, a, c * P:(c + 1) * P],
                                          probs_st[:, a, 16 * b:16 * b + 16], start=(a == 0), stop=(a == 1))
                x.then_inc(s_spv, 1)
                pe.wait_ge(s_whi, 4)
                pe.wait_ge(s_wlo, 4)
                pe.wait_ge(s_slo, 1)
                for s, (m, t) in enumerate(outs):
                    if s >= 4:
                        pe.wait_ge(s_h, s - 3)
                    x = slice(t * THIRD, (t + 1) * THIRD)
                    for k in range(2):
                        w = slice(k * D + m * P, k * D + (m + 1) * P)
                        for p, (a, b) in enumerate(((w_hi, om[0]), (w_hi, om[1]), (w_lo, om[0]))):
                            y = pe.matmul(p_s[:, s % 4, 0:THIRD], a[:, w], b[:, k, x], start=(k == 0 and p == 0), stop=(k == 1 and p == 2))
                    y.then_inc(s_y, 1)
                pe.wait_ge(s_sq, 3)
                pe.wait_ge(s_acc, len(outs) - 3)
                root.tensor(pe)


def feed_forward(nc, d, h_t, n, inv):
    ctx = ExitStack()
    with ctx:
        sb, ps, sem = alloc(nc, ctx)
        ident = sb("ident8", [P, P])
        ones = sb("ones8", [P, P])
        gain = sb("gain8", [P, 2, KC])
        g_raw = sb("g_raw", [P, 2, 2, D])
        g_hi = sb("g_hi", [P, 2, 2, D], F32R)
        g_lo = sb("g_lo", [P, 2, 2, D], F32R)
        o_raw = sb("o_raw", [P, 2, D])
        o_hi = sb("o_hi8", [P, 2, D], F32R)
        o_lo = sb("o_lo8", [P, 2, D], F32R)
        silu = sb("silu", [P, 2, THIRD])
        prod = sb("prod8", [P, 2, THIRD])
        a_hi = sb("a_hi8", [P, 3, 3, THIRD], F32R)
        a_lo = sb("a_lo8", [P, 3, 3, THIRD], F32R)
        flat = g_raw[:, :, :, :].rearrange("p u e c -> p (u e c)")
        acc, sq = (flat[:, T * x:T * x + T].rearrange("p (a c) -> p a c", a=3) for x in range(2))
        mean = o_raw[:, :, :].rearrange("p u c -> p (u c)")[:, 0:T].rearrange("p (a c) -> p a c", a=3)
        y_row = g_raw[:, 0, :, :]
        p_g = ps("p_g8", [P, 3, 2, 512])
        p_y = ps("p_y8", [P, 2, 512])

        normed = NormedRows("g_r", sem, h_t, gain[:, 0, :], inv, n, prod)
        s_const = sem("g_const")
        s_gain = sem("g_gain")
        s_rg = [sem(f"g_rg{u}") for u in range(2)]
        s_ro = [sem(f"g_ro{u}") for u in range(2)]
        s_ghi, s_glo, s_ohi, s_olo = sem("g_ghi"), sem("g_glo"), sem("g_ohi"), sem("g_olo")
        s_gu = sem("g_gu")
        s_silu = sem("g_silu")
        s_prod = sem("g_prod")
        s_ahi = sem("g_ahi")
        s_alo = sem("g_alo")
        s_y = sem("g_y")
        s_h = sem("g_h")
        s_sq = sem("g_sq")
        s_acc = sem("g_acc")
        s_sum, s_mean, s_root, s_inv, s_n = sem("g_sum"), sem("g_mean"), sem("g_root"), sem("g_inv"), sem("g_n")
        s_t, s_tA, s_tD = sem("g_t"), sem("g_tA"), sem("g_tD")
        s_out = [sem(f"g_out{u}") for u in range(2)]

        OUTS = 3 * KC
        PAIRS = FC // 2

        def steps(eng, body):
            def pair(j, parity):
                body(j, 0, parity)
                body(j, 1, 2)

            pair(0, 0)
            pair(1, 1)
            with eng.Fori(1, PAIRS // 2) as i:
                pair(2 * i, 0)
                pair(2 * i + 1, 1)
            pair(PAIRS - 1, 0)

        def pair_is(j, *those):
            return isinstance(j, int) and j in those

        def first(j, u):
            return pair_is(j, 0) and u == 0

        def final(j, u):
            return pair_is(j, PAIRS - 1) and u == 1

        with nc.Block() as block:
            @block.sync
            def _(sp):
                win = d["w_ffn_in"][0].rearrange("(k p) c -> p k c", p=P)

                def load(j, u, slot):
                    f = 2 * j + u
                    if not pair_is(j, 0):
                        sp.wait_ge(s_ghi, f - 1)
                        sp.wait_ge(s_glo, f - 1)
                    for e in range(2):
                        sp.dma_start(g_raw[:, u, e, :].rearrange("p (k c) -> p k c", k=KC), win[:, :, bass.ds(f * P + DFF * e, P)]).then_inc(s_rg[u], 16)
                    if u:
                        for v in range(2):
                            if not pair_is(j, 0):
                                sp.wait_ge(s_ohi, 2 * j - 1 + v)
                                sp.wait_ge(s_olo, 2 * j - 1 + v)
                            sp.dma_start(o_raw[:, v, :], d["w_ffn_out"][0, bass.ds((2 * j + v) * P, P), :]).then_inc(s_ro[v], 16)

                sp.dma_start(gain[:, 0, :], d["g_ffn"][0].rearrange("(k p) -> p k", p=P), allow_slow_non_contiguous=True).then_inc(s_gain, 16)
                steps(sp, load)
                sp.dma_start(ident[:, :], d["ident"]).then_inc(s_const, 16)
                sp.dma_start(ones[:, :], d["ones"]).then_inc(s_const, 16)
                sp.dma_start(gain[:, 1, :], d["g_final"].rearrange("(k p) -> p k", p=P), allow_slow_non_contiguous=True).then_inc(s_const, 16)
                for i in range(TILES):
                    r0, r = i * P, (NS if i == NT else P)
                    sp.wait_ge(s_tA, i + 1)
                    sp.wait_ge(s_tD, i + 1)
                    sp.dma_start(d["y_sample"] if i == NT else d["y_prompt"][r0:r0 + r, :], y_row[0:r, i % 2, :]).then_inc(s_out[i % 2], 16)
                for u in range(2):
                    sp.wait_ge(s_out[u], 16 * ((TILES + 1 - u) // 2))

            @block.scalar
            def _(act):
                def split_gate(j, u):
                    f = 2 * j + u
                    act.wait_ge(s_rg[u], 32 * (j + 1))
                    if not pair_is(j, 0):
                        act.wait_ge(s_gu, 3 * (f - 1))
                    act.activation(g_hi[:, u, :, :], g_raw[:, u, :, :], ACT.Copy).then_inc(s_ghi, 1)

                def split_out(j):
                    for u in range(2):
                        act.wait_ge(s_ro[u], 16 * (j + 1))
                        if not pair_is(j, 0):
                            act.wait_ge(s_y, OUTS * j)
                        act.activation(o_hi[:, u, :], o_raw[:, u, :], ACT.Copy).then_inc(s_ohi, 1)

                def step(j, u, slot):
                    f = 2 * j + u
                    if not final(j, u):
                        split_gate(j + u, 1 - u)
                    if u:
                        split_out(j)
                    for t in range(3):
                        act.wait_ge(s_gu, 3 * f + t + 1)
                        if not first(j, u) or t == 2:
                            act.wait_ge(s_prod, 3 * f + t - 1)
                        act.activation(silu[:, (u + t) % 2, :], p_g[:, t, 0, 0:THIRD], ACT.Silu).then_inc(s_silu, 1)
                        act.wait_ge(s_prod, 3 * f + t + 1)
                        act.activation(a_hi[:, slot, t, :], prod[:, (u + t) % 2, :], ACT.Copy).then_inc(s_ahi, 1)

                split_gate(0, 0)
                for t in range(3):
                    normed.scalar(act, t)
                steps(act, step)
                act.wait_ge(s_prod, 3 * FC)
                act.wait_ge(s_alo, 3 * FC)
                for q in range(OUTS):
                    t = q % 3
                    act.wait_ge(s_h, OUTS * (PAIRS - 1) + q + 1)
                    h = h_t[:, q // 3, t * THIRD:(t + 1) * THIRD]
                    if q < 3:
                        act.activation(acc[:, t, :], h, ACT.Square).then_inc(s_sq, 1)
                    else:
                        if q >= 6:
                            act.wait_ge(s_acc, q - 5)
                        act.activation(sq[:, t, :], h, ACT.Square).then_inc(s_sq, 1)
                for t in range(3):
                    act.wait_ge(s_mean, t + 1)
                    act.activation(mean[:, t, :], mean[:, t, :], ACT.Sqrt).then_inc(s_root, 1)
                for i in range(TILES):
                    r = NS if i == NT else P
                    act.wait_ge(s_t, i + 1)
                    if i >= 2:
                        act.wait_ge(s_out[i % 2], 16 * (i // 2))
                    act.activation(y_row[0:r, i % 2, 0:512], p_g[0:r, i % 2, 0, :], ACT.Copy).then_inc(s_tA, 1)

            @block.gpsimd
            def _(pool):
                for q in range(3, OUTS):
                    pool.wait_ge(s_sq, q + 1)
                    if q >= 6:
                        pool.wait_ge(s_acc, q - 5)
                    pool.tensor_tensor(acc[:, q % 3, :], acc[:, q % 3, :], sq[:, q % 3, :], ALU.add).then_inc(s_acc, 1)

            @block.vector
            def _(dve):
                def split_gate(f, u):
                    dve.wait_ge(s_ghi, f + 1)
                    dve.tensor_tensor(g_lo[:, u, :, :], g_raw[:, u, :, :], g_hi[:, u, :, :].bitcast(F32), ALU.subtract).then_inc(s_glo, 1)

                def split_out(j):
                    for u in range(2):
                        dve.wait_ge(s_ohi, 2 * j + u + 1)
                        dve.tensor_tensor(o_lo[:, u, :], o_raw[:, u, :], o_hi[:, u, :].bitcast(F32), ALU.subtract).then_inc(s_olo, 1)

                def take_out(j):
                    if not pair_is(j, 0):
                        dve.wait_ge(s_h, OUTS * j)
                    for q in range(OUTS):
                        h = h_t[:, q // 3, q % 3 * THIRD:(q % 3 + 1) * THIRD]
                        dve.wait_ge(s_y, OUTS * j + q + 1)
                        dve.tensor_tensor(h, h, p_y[:, q % 2, 0:THIRD], ALU.add).then_inc(s_h, 1)

                def step(j, u, slot):
                    f = 2 * j + u
                    if not final(j, u):
                        split_gate(f + 1, 1 - u)
                    if u:
                        split_out(j)
                    for t in range(3):
                        dve.wait_ge(s_silu, 3 * f + t + 1)
                        if not first(j, u) or t == 2:
                            dve.wait_ge(s_alo, 3 * f + t - 1)
                        dve.tensor_tensor(prod[:, (u + t) % 2, :], silu[:, (u + t) % 2, :], p_g[:, t, 1, 0:THIRD], ALU.mult).then_inc(s_prod, 1)
                        dve.wait_ge(s_ahi, 3 * f + t + 1)
                        dve.tensor_tensor(a_lo[:, slot, t, :], prod[:, (u + t) % 2, :], a_hi[:, slot, t, :].bitcast(F32), ALU.subtract).then_inc(s_alo, 1)
                    if u == 0 and not pair_is(j, 0):
                        take_out(j - 1)

                split_gate(0, 0)
                dve.wait_ge(s_gain, 16)
                for t in range(3):
                    normed.vector(dve, t)
                dve.wait_ge(normed.s_lo, 3 * KC)
                steps(dve, step)
                take_out(PAIRS - 1)
                dve.wait_ge(s_const, 48)
                for t in range(3):
                    dve.wait_ge(s_sum, t + 1)
                    dve.tensor_scalar(mean[:, t, :], p_y[:, t % 2, 0:THIRD], 1.0 / D, EPS, ALU.mult, ALU.add).then_inc(s_mean, 1)
                for t in range(3):
                    dve.wait_ge(s_root, t + 1)
                    dve.reciprocal(mean[:, t, :], mean[:, t, :]).then_inc(s_inv, 1)
                    dve.wait_ge(s_inv, t + 1)
                    for k in range(KC):
                        h = h_t[:, k, t * THIRD:(t + 1) * THIRD]
                        e = dve.scalar_tensor_tensor(out=h, in0=h, scalar=gain[:, 1, k:k + 1], in1=mean[:, t, :], op0=ALU.mult, op1=ALU.mult)
                    e.then_inc(s_n, 1)
                for i in range(TILES):
                    r = NS if i == NT else P
                    dve.wait_ge(s_t, i + 1)
                    if i >= 2:
                        dve.wait_ge(s_out[i % 2], 16 * (i // 2))
                    dve.tensor_copy(y_row[0:r, i % 2, 512:D], p_g[0:r, i % 2, 1, :]).then_inc(s_tD, 1)

            @block.tensor
            def _(pe):
                def gate_up(j, u):
                    f = 2 * j + u
                    pe.wait_ge(s_ghi, f + 1)
                    pe.wait_ge(s_glo, f + 1)
                    for t in range(3):
                        if first(j, u):
                            pe.wait_ge(normed.s_lo, KC * (t + 1))
                        else:
                            pe.wait_ge(s_prod, 3 * f + t - 2)
                        for e in range(2):
                            for k in range(KC):
                                w = slice(k * P, (k + 1) * P)
                                for p, (a, b) in enumerate(((g_hi, n[0]), (g_hi, n[1]), (g_lo, n[0]))):
                                    m = pe.matmul(p_g[:, t, e, 0:THIRD], a[:, u, e, w], b[:, k, t * THIRD:(t + 1) * THIRD],
                                                  start=(k == 0 and p == 0), stop=(k == KC - 1 and p == 2))
                        m.then_inc(s_gu, 1)

                def out(j, parity):
                    pe.wait_ge(s_ohi, 2 * j + 2)
                    pe.wait_ge(s_olo, 2 * j + 2)
                    pe.wait_ge(s_alo, 6 * j + 6)
                    for q in range(OUTS):
                        m, t = q // 3, q % 3
                        if not (pair_is(j, 0) and q < 2):
                            pe.wait_ge(s_h, OUTS * j + q - 1)
                        w = slice(m * P, (m + 1) * P)
                        for u in range(2):
                            for p, (a, b) in enumerate(((o_hi, a_hi), (o_hi, a_lo), (o_lo, a_hi))):
                                y = pe.matmul(p_y[:, q % 2, 0:THIRD], a[:, u, w], b[:, 2 if u else parity, t, :], start=(u == 0 and p == 0), stop=(u == 1 and p == 2))
                        y.then_inc(s_y, 1)

                def step(j, u, slot):
                    gate_up(j, u)
                    if u == 0 and not pair_is(j, 0):
                        out(j - 1, 1 - slot)

                steps(pe, step)
                out(PAIRS - 1, (PAIRS - 1) % 2)
                pe.wait_ge(s_const, 48)
                pe.wait_ge(s_sq, 3)
                pe.wait_ge(s_acc, OUTS - 3)
                for t in range(3):
                    if t < 2:
                        pe.wait_ge(s_h, OUTS * PAIRS)
                    else:
                        pe.wait_ge(s_mean, t - 1)
                    pe.matmul(p_y[:, t % 2, 0:THIRD], ones[:, :], acc[:, t, :], start=True, stop=True).then_inc(s_sum, 1)
                for i in range(TILES):
                    r = NS if i == NT else P
                    pe.wait_ge(s_n, min(3, (i * P + r - 1) // THIRD + 1))
                    if i >= 2:
                        pe.wait_ge(s_tA, i - 1)
                        pe.wait_ge(s_tD, i - 1)
                    for k in range(KC):
                        m = pe.transpose(p_g[0:r, i % 2, k // 4, k % 4 * P:(k % 4 + 1) * P], h_t[:, k, i * P:i * P + r], ident[:, :])
                    m.then_inc(s_t, 1)


def run_phases(nc, d):
    with ExitStack() as outer:
        def on(stack, name, shape, dt=F32, side="left"):
            return stack.enter_context(nc.sbuf_tensor(name, shape, dt, side=side))

        with ExitStack() as mixers:
            with ExitStack() as choice:
                sel = on(choice, "sel", [P, SEL_COLS], side="right")
                project_and_select(nc, d, sel)
                oa = [on(mixers, f"oa_{x}", [P, 4, T], F32R) for x in ("hi", "lo")]
                kv_pages = on(choice, "kv_pages", [P, PAGED, NPG, 2 * P], side="right")
                attend_prompt(nc, d, sel, oa, kv_pages)
                ob = [on(mixers, f"ob_{x}", [P, 2, T], F32R) for x in ("hi", "lo")]
                attend_sample_a(nc, d, sel, oa, ob, kv_pages)
            inv_ffn = on(outer, "inv_ffn", [P, T], side="right")
            km_t = inv_ffn[:, 0:4 * P].rearrange("p (c k) -> p c k", c=2)
            vm = inv_ffn[:, 4 * P:8 * P].rearrange("p (c k) -> p c k", c=2)
            with ExitStack() as loaded:
                m_in = on(loaded, "m_in", [P, 2, D], side="right")
                w_raw = on(loaded, "w_mem_raw", [P, KC, 512], side="right")
                attend_sample_b(nc, d, ob, m_in, w_raw)
                mem_project(nc, d, km_t, vm, m_in, w_raw)
            h_t = on(outer, "h_t", [P, KC, T], side="right")
            n = [on(outer, f"n_t_{x}", [P, KC, T], F32R, side="right") for x in ("hi", "lo")]
            before = outer.enter_context(ExitStack())
            inv_mem = on(before, "inv_mem", [P, T], side="right")
            merge(nc, d, oa, ob, h_t, n, inv_mem)
        attend_mem(nc, d, km_t, vm, h_t, n, inv_mem, inv_ffn)
        before.close()
        feed_forward(nc, d, h_t, n, inv_ffn)


_INS = ["x_prompt", "x_sample", "mem_prompt", "cache_attn_kv", "cache_idx_k", "cache_win1_kv", "cache_win2_kv",
        "cache_win3_kv", "cache_mem_kv", "page_table", "g_mix", "w_in", "w_br_a", "w_br_b", "w_out", "g_mem",
        "w_mem_q", "w_mem_kv", "w_mem_o", "g_ffn", "w_ffn_in", "w_ffn_out", "g_final"]
_OUTS = [("y_prompt", (1, SEQ, D)), ("y_sample", (DB, DS, D)), ("new_kv_prompt", (1, 1, SEQ, 2, AKV, HD)),
         ("new_idx_k_prompt", (1, 1, SEQ, HD)), ("new_win1_prompt", (1, 1, 128, 2, BH, HD)),
         ("new_win2_prompt", (1, 1, 512, 2, BH, HD)), ("new_win3_prompt", (1, 1, SEQ, 2, BH, HD)),
         ("new_mem_kv_prompt", (1, 1, MEMT, 2, BH, HD)), ("new_kv_sample", (1, DB, DS, 2, AKV, HD)),
         ("new_idx_k_sample", (1, DB, DS, HD)), ("new_win1_sample", (1, DB, 128, 2, BH, HD)),
         ("new_win2_sample", (1, DB, 512, 2, BH, HD)), ("new_win3_sample", (1, DB, PAST + DS, 2, BH, HD))]


def build(nc, a, o):
    d = {k: a[k] for k in ("w_in", "g_mix", "g_mem", "g_ffn", "w_br_a", "w_br_b", "w_out", "w_mem_q", "w_mem_kv",
                           "w_mem_o", "w_ffn_in", "w_ffn_out", "g_final", "page_table", *constants())}
    d["n_phys"] = a["cache_idx_k"].shape[1]
    d["x_prompt"] = a["x_prompt"].rearrange("a t c -> (a t) c")
    d["x_sample"] = a["x_sample"].rearrange("b t c -> (b t) c")
    d["mem_prompt"] = a["mem_prompt"].rearrange("a t c -> (a t) c")
    d["cache_attn_kv"] = a["cache_attn_kv"].rearrange("l n p s h e -> (l n) p (s h e)")
    d["cache_idx_k"] = a["cache_idx_k"].rearrange("l n p e -> (l n) p e")
    d["cache_win"] = [a[f"cache_win{g}_kv"].rearrange("l b r s h e -> (l b) r (s h e)") for g in (1, 2, 3)]
    d["cache_mem_kv"] = a["cache_mem_kv"].rearrange("l b r s h e -> (l b) r (s h e)")
    d["y_prompt"] = o["y_prompt"].rearrange("a t c -> (a t) c")
    d["y_sample"] = o["y_sample"].rearrange("b t c -> (b t) c")
    d["new_kv_prompt"] = o["new_kv_prompt"].rearrange("l b t s h e -> (l b t) (s h e)")
    d["new_kv_sample"] = o["new_kv_sample"].rearrange("l b t s h e -> (l b t) (s h e)")
    d["new_idx_k_prompt"] = o["new_idx_k_prompt"].rearrange("l b t e -> (l b t) e")
    d["new_idx_k_sample"] = o["new_idx_k_sample"].rearrange("l b t e -> (l b t) e")
    d["new_win_prompt"] = [o[f"new_win{g}_prompt"].rearrange("l b t s h e -> (l b t) (s h e)") for g in (1, 2, 3)]
    d["new_win_sample"] = [o[f"new_win{g}_sample"].rearrange("l b t s h e -> (l b) t (s h e)") for g in (1, 2, 3)]
    d["new_mem_kv"] = o["new_mem_kv_prompt"].rearrange("l b t s h e -> (l b t) (s h e)")

    def scratch(name, shape):
        return nc.dram_tensor(name, shape, F32).ap()

    d["z_qi"] = scratch("z_qi", (NS, IH * HD))
    d["z_wi"] = scratch("z_wi", (NS, IH))
    d["z_qa"] = scratch("z_qa", (NS, AH * HD))
    d["z_qb"] = [scratch(f"z_qb{g}", (NS, BH * HD)) for g in range(3)]
    d["z_a"] = scratch("z_a", (T, ZB))
    d["z_b"] = [scratch(f"z_b{g}", (T, ZB)) for g in range(3)]
    d["gates"] = scratch("gates", (2 * D, T))
    d["o_b"] = [scratch(f"o_b{g}", (SEQ, 264)) for g in range(3)]
    d["o_s"] = scratch("o_s", (NS, 512))
    run_phases(nc, d)


def kernel(**inputs):
    import numpy as _np
    import concourse.bacc as _bacc
    from concourse import mybir as _mybir
    from concourse.bass_utils import run_bass_kernel_spmd as _run

    nc = _bacc.Bacc("TRN2", target_bir_lowering=False, num_devices=1)
    arrays, a, o = {}, {}, {}
    for name, value in [(n, inputs[n]) for n in _INS] + list(constants().items()):
        v = _np.ascontiguousarray(value)
        arrays[f"in_{name}"] = v
        a[name] = nc.dram_tensor(f"in_{name}", v.shape, _mybir.dt.from_np(v.dtype), kind="ExternalInput").ap()
    for name, shape in _OUTS:
        o[name] = nc.dram_tensor(f"out_{name}", shape, F32, kind="ExternalOutput").ap()
    build(nc, a, o)
    r = _run(nc, [arrays], core_ids=[0])
    return tuple(r.results[0][f"out_{name}"] for name, _ in _OUTS)
```
